# Optimizing a Trainium2 kernel written in Bass

```python
import math
import jax, jax.numpy as jnp
from jax import lax
import numpy as np

D_MODEL = 1024
BATCH = 1
SEQ = 256
DEPTH = 1
DEC_BATCH = 8
DEC_SEQ = 8
PAST_LEN = 2048
PAGE_SIZE = 128

D_MIX = D_MODEL
D_CONV = D_MIX // 2
D_HGRN = D_MIX - D_CONV
CONV_WIDTH = 3
CONV_GROUPS = 8
HGRN_EXPAND = 128
HGRN_HEADS = D_HGRN // HGRN_EXPAND
DK = HGRN_EXPAND
DV = D_HGRN // HGRN_HEADS
CHUNK = 64
N_EXPERTS = 32
TOP_K = 4
D_FF = D_MODEL
SWIGLU_LIMIT = 7.0
SWIGLU_ALPHA = 1.702
EPS = 1e-6
D_PROJ = 3 * D_CONV + 4 * D_HGRN

kernel_name = "hybrid_shortconv_hgrn2_moe_step"

def rmsnorm(x, w):
    xf = x.astype(jnp.float32)
    y = xf * lax.rsqrt(jnp.mean(xf * xf, axis=-1, keepdims=True) + EPS)
    return (y * w.astype(jnp.float32)).astype(x.dtype)

def short_conv(u, buf, conv_w, conv_b):
    L = u.shape[1]
    upad = jnp.concatenate([buf.astype(u.dtype), u], axis=1)
    out = (conv_w[0] * upad[:, 0:L] + conv_w[1] * upad[:, 1:L + 1]
           + conv_w[2] * upad[:, 2:L + 2] + conv_b)
    return out, upad[:, -(CONV_WIDTH - 1):]

def hgrn2_chunked(q, logf, k, v, s0):
    B, L, H, _ = q.shape
    c = math.gcd(CHUNK, L)
    n = L // c

    def blocks(a):
        return a.reshape(B, n, c, H, a.shape[-1]).transpose(1, 0, 2, 3, 4)

    mask = jnp.tril(jnp.ones((c, c), dtype=bool))[None, :, :, None, None]

    def step(S, inp):
        qc, lfc, kc, vc = inp
        A = jnp.cumsum(lfc, axis=1)
        inter = jnp.einsum('bthk,bhkv->bthv', qc * jnp.exp(A), S)
        diff = A[:, :, None] - A[:, None, :]
        decay = jnp.exp(jnp.where(mask, diff, -jnp.inf))
        scores = jnp.einsum('bthk,bshk,btshk->bths', qc, kc, decay)
        intra = jnp.einsum('bths,bshv->bthv', scores, vc)
        AL = A[:, -1]
        S_new = (jnp.exp(AL)[..., None] * S
                 + jnp.einsum('bshk,bshv->bhkv', kc * jnp.exp(AL[:, None] - A), vc))
        return S_new, inter + intra

    S_fin, o = lax.scan(step, s0, (blocks(q), blocks(logf), blocks(k), blocks(v)))
    o = o.transpose(1, 0, 2, 3, 4).reshape(B, L, H, DV)
    return o, S_fin

def moe(h, router_w, router_b, w_gate, b_gate, w_up, b_up, w_down, b_down):
    Bsz, L, D = h.shape
    t = h.reshape(Bsz * L, D)
    logits = (t @ router_w + router_b).astype(jnp.float32)
    vals, idx = lax.top_k(logits, TOP_K)
    gates = jax.nn.softmax(vals, axis=-1)
    combine = jnp.einsum('tk,tke->te', gates, jax.nn.one_hot(idx, N_EXPERTS, dtype=jnp.float32))
    y = jnp.zeros((Bsz * L, D), jnp.float32)
    for e in range(N_EXPERTS):
        a = jnp.minimum((t @ w_gate[e] + b_gate[e]).astype(jnp.float32), SWIGLU_LIMIT)
        u = jnp.clip((t @ w_up[e] + b_up[e]).astype(jnp.float32), -SWIGLU_LIMIT, SWIGLU_LIMIT)
        hid = ((u + 1.0) * a * jax.nn.sigmoid(SWIGLU_ALPHA * a)).astype(t.dtype)
        y = y + combine[:, e:e + 1] * (hid @ w_down[e] + b_down[e]).astype(jnp.float32)
    return y.astype(h.dtype).reshape(Bsz, L, D)

def layer(x, conv_state, hgrn_state, lb, norm_mix_w, w_in, conv_w, conv_b, gnorm_w, w_out,
          norm_ffn_w, router_w, router_b, w_gate, b_gate, w_up, b_up, w_down, b_down):
    B, L, _ = x.shape
    h = rmsnorm(x, norm_mix_w)
    proj = h @ w_in
    bg, cg, v_c, q, f, i, g = jnp.split(
        proj, np.cumsum([D_CONV, D_CONV, D_CONV, D_HGRN, D_HGRN, D_HGRN])[:].tolist(), axis=-1)
    conv_out, new_conv = short_conv(cg * v_c, conv_state, conv_w, conv_b)
    y_conv = bg * conv_out
    ff = f.astype(jnp.float32)
    lbf = lb.astype(jnp.float32)
    logf = jnp.log(lbf + (1.0 - lbf) * jax.nn.sigmoid(ff))
    k = (1.0 - lbf) * jax.nn.sigmoid(-ff)
    heads = lambda a: a.astype(jnp.float32).reshape(B, L, HGRN_HEADS, -1)
    o, new_hgrn = hgrn2_chunked(heads(q), heads(logf), heads(k), heads(i),
                                hgrn_state.astype(jnp.float32))
    o = o * lax.rsqrt(jnp.mean(o * o, axis=-1, keepdims=True) + EPS)
    o = o.reshape(B, L, D_HGRN) * gnorm_w.astype(jnp.float32) * jax.nn.silu(g.astype(jnp.float32))
    mix = jnp.concatenate([y_conv, o.astype(x.dtype)], axis=-1) @ w_out
    x = x + mix
    x = x + moe(rmsnorm(x, norm_ffn_w), router_w, router_b, w_gate, b_gate, w_up, b_up,
                w_down, b_down)
    return x, new_conv, new_hgrn

def setup_inputs(seed: int = 0) -> dict:
    key = jax.random.key(seed)
    ks = jax.random.split(key, 24)
    nrm = lambda k, s, sc: jax.random.normal(k, s, jnp.float32) * sc
    return {
        "x_prompt": nrm(ks[0], (BATCH, SEQ, D_MODEL), 1.0),
        "x_sample": nrm(ks[1], (DEC_BATCH, DEC_SEQ, D_MODEL), 1.0),
        "state_conv": nrm(ks[2], (DEPTH, DEC_BATCH, CONV_WIDTH - 1, D_CONV), 1.0),
        "state_hgrn": nrm(ks[3], (DEPTH, DEC_BATCH, HGRN_HEADS, DK, DV), 0.3),
        "lb_logits": nrm(ks[4], (DEPTH + 1, D_HGRN), 0.5),
        "norm_mix_w": 1.0 + nrm(ks[5], (DEPTH, D_MODEL), 0.02),
        "w_in": nrm(ks[6], (DEPTH, D_MODEL, D_PROJ), D_MODEL ** -0.5),
        "conv_w": nrm(ks[7], (DEPTH, CONV_WIDTH, D_CONV), CONV_WIDTH ** -0.5),
        "conv_b": nrm(ks[8], (DEPTH, D_CONV), 0.01),
        "gnorm_w": 1.0 + nrm(ks[9], (DEPTH, D_HGRN), 0.02),
        "w_out": nrm(ks[10], (DEPTH, D_MIX, D_MODEL), D_MIX ** -0.5),
        "norm_ffn_w": 1.0 + nrm(ks[11], (DEPTH, D_MODEL), 0.02),
        "router_w": nrm(ks[12], (DEPTH, D_MODEL, N_EXPERTS), D_MODEL ** -0.5),
        "router_b": nrm(ks[13], (DEPTH, N_EXPERTS), 0.01),
        "w_gate": nrm(ks[14], (DEPTH, N_EXPERTS, D_MODEL, D_FF), D_MODEL ** -0.5),
        "b_gate": nrm(ks[15], (DEPTH, N_EXPERTS, D_FF), 0.01),
        "w_up": nrm(ks[16], (DEPTH, N_EXPERTS, D_MODEL, D_FF), D_MODEL ** -0.5),
        "b_up": nrm(ks[17], (DEPTH, N_EXPERTS, D_FF), 0.01),
        "w_down": nrm(ks[18], (DEPTH, N_EXPERTS, D_FF, D_MODEL), D_FF ** -0.5),
        "b_down": nrm(ks[19], (DEPTH, N_EXPERTS, D_MODEL), 0.01),
        "final_norm_w": 1.0 + nrm(ks[20], (D_MODEL,), 0.02),
    }

def reference(x_prompt, x_sample, state_conv, state_hgrn, lb_logits, norm_mix_w, w_in, conv_w,
              conv_b, gnorm_w, w_out, norm_ffn_w, router_w, router_b, w_gate, b_gate, w_up,
              b_up, w_down, b_down, final_norm_w):
    lb_all = jnp.cumsum(jax.nn.softmax(lb_logits.astype(jnp.float32), axis=0), axis=0)
    xp, xs = x_prompt, x_sample
    conv_p, hgrn_p, conv_s, hgrn_s = [], [], [], []
    for l in range(DEPTH):
        w = (norm_mix_w[l], w_in[l], conv_w[l], conv_b[l], gnorm_w[l], w_out[l], norm_ffn_w[l],
             router_w[l], router_b[l], w_gate[l], b_gate[l], w_up[l], b_up[l], w_down[l],
             b_down[l])
        zc = jnp.zeros((BATCH, CONV_WIDTH - 1, D_CONV), x_prompt.dtype)
        zh = jnp.zeros((BATCH, HGRN_HEADS, DK, DV), jnp.float32)
        xp, cp, hp = layer(xp, zc, zh, lb_all[l], *w)
        xs, cs, hs = layer(xs, state_conv[l], state_hgrn[l], lb_all[l], *w)
        conv_p.append(cp)
        hgrn_p.append(hp.astype(x_prompt.dtype))
        conv_s.append(cs.astype(state_conv.dtype))
        hgrn_s.append(hs.astype(state_hgrn.dtype))
    y_prompt = rmsnorm(xp, final_norm_w)
    y_sample = rmsnorm(xs, final_norm_w)
    return (y_prompt, y_sample, jnp.stack(conv_p), jnp.stack(hgrn_p), jnp.stack(conv_s),
            jnp.stack(hgrn_s))


_drawn_inputs = setup_inputs


def setup_inputs(seed=0):
    import zlib

    import numpy as np

    out = dict(_drawn_inputs(seed))
    spreads = {}
    factors = {'b_gate': 8.0, 'b_up': 22.028, 'b_down': 8.0, 'final_norm_w': 8.622}
    for name, (base, spread) in spreads.items():
        noise = np.random.default_rng([zlib.crc32(name.encode()), seed]).standard_normal(out[name].shape)
        drawn = base * np.exp(spread * noise) if base else spread * noise
        out[name] = __import__('jax').numpy.asarray(drawn.astype(out[name].dtype))
    for name, factor in factors.items():
        out[name] = (out[name] * factor).astype(out[name].dtype)
    return out
```

```python
import concourse.bass as bass
from concourse import mybir
from contextlib import ExitStack


def hybrid_shortconv_hgrn2_moe_step(nc, A):
    f32, bf16, u8 = mybir.dt.float32, mybir.dt.bfloat16, mybir.dt.uint8
    i32, u32 = mybir.dt.int32, mybir.dt.uint32
    ALU, ACT, AX = mybir.AluOpType, mybir.ActivationFunctionType, mybir.AxisListType

    D = 1024
    KT = D // 128
    NP, NSEQ, LS = 256, 8, 8
    NT = NP + NSEQ * LS
    TOK = [(0, 128), (128, 128), (256, 64)]
    NH = 4
    E = 32
    SLOTS = 64
    ROUNDS = NT // SLOTS
    TOPK = 4
    LIMIT, ALPHA, EPS = 7.0, 1.702, 1e-6
    NLEV = 7

    NR = 16
    W_CHUNK = {"f": (0, 8), "q": (2, 6), "i": (4, 10), "g": (6, 12), "cg": (10, 2), "vc": (12, 4), "bg": (14, 0)}
    L_S0, L_BIAS, L_WOUT, L_EXP = 8, 16, 18, 22
    LPE = 12
    PER_BODY = 4
    BODIES = E // PER_BODY
    NO_RING_SEM = {0, 1, 8, 9}

    def ring_value(L):
        special = (L_S0, L_S0 + 1, L_BIAS, L_BIAS + 1)
        return 16 * sum(1 for q in range(L % NR, L + 1, NR) if q not in special)

    UNITS = ([("f", h) for h in range(NH)] + [("q", h) for h in range(NH)]
             + [("i", c, b) for c in range(2) for b in range(3)] + [("g", h) for h in range(NH)]
             + [("cg", c) for c in range(NH)] + [("vc", c) for c in range(NH)] + [("bg", c) for c in range(NH)])
    UIDX = {u: n for n, u in enumerate(UNITS)}
    STEPS = [("lev", l, p) for l in range(NLEV + 1) for p in range(2)] + [("cross",)] + [("o", h) for h in range(NH)]
    SCHED = []
    left = list(STEPS)
    for n, u in enumerate(UNITS):
        SCHED.append(u)
        if n >= 8 and left:
            SCHED.append(left.pop(0))
    SCHED += left

    def load_done(L):
        for kind, (l0, _) in W_CHUNK.items():
            if l0 <= L < l0 + 2:
                return 1 + (UIDX[(kind, L - l0, 2)] if kind == "i" else UIDX[(kind, 2 * (L - l0) + 1)])

    ctx = ExitStack()
    with ctx:
        def sb(name, shape, dt=f32):
            return ctx.enter_context(nc.sbuf_tensor(name, shape, dt))

        def sem(name):
            return ctx.enter_context(nc.semaphore(name))

        ring = sb("ring", [128, NR, 2048])
        x = sb("x", [128, 3, D])
        R1 = sb("R1", [128, 5120])
        R2 = sb("R2", [128, 2560])
        R3 = sb("R3", [128, 4608])
        R4 = sb("R4", [128, 2632])

        def view(region, at, pattern=None, **kw):
            n = 1
            for v in kw.pop("shape"):
                n *= v
            ap = region[:, at:at + n]
            return ap.rearrange(pattern, **kw) if pattern else ap

        hT = view(R1, 0, "p (k t) -> p k t", shape=(8, NT), k=8)
        qP = view(R1, 2560, "p (h t) -> p h t", shape=(4, NT), h=4)
        kS = view(R1, 3840, "p (h t) -> p h t", shape=(4, NT), h=4)
        kTok = view(R1, 0, "p (n d) -> p n d", shape=(12, 128), n=12)
        vSel = [view(R1, at, "p (b d) -> p b d", shape=(8, 128), b=8) for at in (1536, 2560)]
        h2p = R1[:, 0:4608].bitcast(bf16).rearrange("p (s b d) -> p s b d", s=3, b=3)
        yout = view(R1, 0, "p (b d) -> p b d", shape=(3, D), b=3)
        junk2 = view(R1, 3072, shape=(D,))
        mixT = view(R2, 0, "p (k t) -> p k t", shape=(8, NT), k=8)
        fdec = view(R2, 0, "p (h t) -> p h t", shape=(4, NT), h=4)
        q = view(R2, 1280, "p (h t) -> p h t", shape=(4, NT), h=4)
        fnw = view(R2, 0, shape=(D,))
        g = view(R3, 0, "p (h t) -> p h t", shape=(4, NT), h=4)
        sc = view(R3, 1280, "p (h t) -> p h t", shape=(4, 448), h=4)
        v = view(R3, 3072, "p (b d) -> p b d", shape=(3, 512), b=3)
        hs = view(R3, 0, "p (b d) -> p b d", shape=(3, D), b=3)
        histRows = view(R3, 3072, shape=(512,))
        maskIn = view(R3, 3584, "p (l t) -> p l t", shape=(NLEV, 128), l=NLEV)
        h2f = view(R3, 0, "p (b d) -> p b d", shape=(2, D), b=2)
        stP = view(R3, 2048, "p (h d) -> p h d", shape=(4, 128), h=4)
        tailT = view(R3, 2560, shape=(512,))
        x2T = view(R3, 3072, "p (k t) -> p k t", shape=(8, 128), k=8)
        ga, gs, gu, gt, xgs, xgT, hidT, ysb, hid = [view(R3, 512 * n, shape=(512,)) for n in range(9)]
        cv = view(R4, 0, "p (c t) -> p c t", shape=(4, NT), c=4)
        u = view(R4, 1280, "p (c t) -> p c t", shape=(4, NT + 2 + 2 * NSEQ), c=4)
        junk = view(R4, 0, shape=(D,))
        tail = view(R4, 0, "p (c t) -> p c t", shape=(4, 18), c=4)
        bias3 = R4[:, 0:1536].bitcast(bf16).rearrange("p (m d) -> p m d", m=3)
        G = view(R4, 1536, "p (b s) -> p b s", shape=(3, 128), b=3)
        GT = view(R4, 1920, "p (n t) -> p n t", shape=(2, NT), n=2)

        consts = sb("consts", [128, 128 * 4 + 34 + 8 + 8 + 32])
        ident, tri, ones, iota2 = [consts[:, 128 * n:128 * n + 128] for n in range(4)]
        expCol = consts[:, 512:546]
        roundStart = consts[:, 546:554]
        seqMask = consts[:, 554:562]
        expId = consts[:, 562:594]
        levMask = sb("levMask", [128, NLEV, 128], u8)
        trib = sb("trib", [128, 128], bf16)
        onesb = sb("onesb", [128, 128], bf16)
        rw = sb("rw", [128, 8, E])
        rb = sb("rb", [128, E])
        parRows = sb("parRows", [44, 128])
        par = sb("par", [128, 44])
        lbW = sb("lbW", [128, 5, 4])
        lb = sb("lb", [128, 4])
        oml = sb("oml", [128, 4])
        epsT = sb("epsT", [128, 1])
        st = sb("st", [128, 24])
        f8 = sb("f8", [128, 4, NSEQ])
        lg = sb("lg", [128, 3, E])
        mx = sb("mx", [128, 3, 8])
        mi = sb("mi", [128, 3, 8], u32)
        mif = sb("mif", [128, 3, 8])
        ex = sb("ex", [128, 3, 4])
        oh = sb("oh", [128, 2, E])
        comb = sb("comb", [128, 3, E + 1])
        sel = sb("sel", [128, 3, E], bf16)
        posm = sb("posm", [128, 3, E + 1])
        cmax = sb("cmax", [128, 1])
        flag = sb("flag", [128, 8], i32)
        P = sb("P", [128, 3, SLOTS], bf16)
        eh = sb("eh", [128, 2, SLOTS], bf16)

        ps = ctx.enter_context(nc.psum_tensor("ps", [128, 8, 512], f32))

        def banks(a, n, rows, cols):
            return ps[0:rows, a:a + n, 0:cols]

        ringIn = [sem(f"ring_in{s}") for s in range(NR)]
        xIn = [sem(f"x_in{b}") for b in range(3)]
        constIn, parIn, routerIn, histIn = sem("const_in"), sem("par_in"), sem("router_in"), sem("hist_in")
        s0In, biasIn, fnwIn = sem("s0_in"), sem("bias_in"), sem("fnw_in")
        s0Out, stOut, tailOut, yOut = sem("s0_out"), sem("state_out"), sem("tail_out"), sem("y_out")
        parMM, xTMM, projMM, levMM, oMM = sem("par_mm"), sem("xT_mm"), sem("proj_mm"), sem("lev_mm"), sem("o_mm")
        ssMM, kTokMM, stPMM, stSMM, tailMM = sem("ss_mm"), sem("ktok_mm"), sem("stp_mm"), sem("sts_mm"), sem("tail_mm")
        woutMM, x2TMM, lgMM, posMM = sem("wout_mm"), sem("x2T_mm"), sem("lg_mm"), sem("pos_mm")
        wUsed = sem("w_used")
        xgMM, gtMM, xgTMM, hidTMM, scatMM = sem("xg_mm"), sem("gt_mm"), sem("xgT_mm"), sem("hidT_mm"), sem("scat_mm")
        unitOut = [sem(f"unit_out{n}") for n in range(2)]
        ssqDone, rootDone, expDone = sem("ssq_done"), sem("root_done"), sem("lbexp_done")
        gSig, crossOut, oSq, oRoot = sem("gsig"), sem("cross_out"), sem("osq"), sem("oroot")
        kTokOut, tailTOut = sem("ktok_out"), sem("tailT_out")
        ssq2Done, root2Done, x2TOut, exDone, partDone = (sem("ssq2"), sem("root2"), sem("x2T_out"), sem("ex_done"),
                                                          sem("part_done"))
        sigDone, xgOut, gtOut, hidTOut, yEvac = sem("sig_done"), sem("xg_out"), sem("gt_out"), sem("hidT_out"), sem("y_evac")
        finSq, finRoot = sem("fin_sq"), sem("fin_root")
        step = sem("dve_step")
        parOut, hsDone, hTOut, levOut, kScaled = sem("par_out"), sem("hs_done"), sem("hT_out"), sem("lev_out"), sem("k_scaled")
        f8Out, mixDone, stPOut, stSOut = sem("f8_out"), sem("mix_done"), sem("stp_out"), sem("sts_out")
        x2Done, resid, lgOut, mxDone, selDone, posOut = (sem("x2_done"), sem("resid"), sem("lg_out"), sem("mx_done"),
                                                         sem("sel_done"), sem("pos_out"))
        h2Parts, flagDone, histOut, epsOut, maskOut = sem("h2_parts"), sem("flag_done"), sem("hist_out"), sem("eps_out"), sem("mask_out")
        prep, aDone, uDone, tDone, hidDone, xgTOut, accDone = (sem("prep"), sem("a_done"), sem("u_done"), sem("t_done"),
                                                               sem("hid_done"), sem("xgT_out"), sem("acc_done"))
        posShift, moeDone, finDone = sem("pos_shift"), sem("moe_done"), sem("fin_done")
        aloneP, aloneV, aloneT = sem("alone_pool"), sem("alone_dve"), sem("alone_pe")
        vSelDone, s0Scaled, tailIn, biasDone, biasStep, ehDone = (sem("vsel_done"), sem("s0_scaled"), sem("tail_in"),
                                                                  sem("bias_done"), sem("bias_step"), sem("eh_done"))

        w_in = A["w_in"][0].rearrange("(k p) n -> p k n", p=128)
        w_out = A["w_out"][0].rearrange("(k p) n -> p k n", p=128)
        w_exp = [A[n][0].rearrange("e (k p) n -> e p k n", p=128) for n in ("w_gate", "w_up", "w_down")]
        b_exp = [A[n][0] for n in ("b_gate", "b_up", "b_down")]
        s0 = ring[:, L_S0:L_S0 + 2, :].rearrange("p s (n d) -> p (s n) d", d=128)
        s0v = s0.rearrange("p (b h) d -> p b h d", h=NH)
        biasRaw = ring[:, L_BIAS % NR:L_BIAS % NR + 2, :].rearrange("p s n -> p (s n)")

        def slot_k(L, cols):
            return ring[:, L % NR, :].rearrange("p (k n) -> p k n", n=cols)

        START = 1

        def credit(eng, *sems):
            for s in sems:
                eng.sem_inc(s, START)

        block = ctx.enter_context(nc.Block())

        @block.sync
        def _(sp):
            def load_expert(e, j, s):
                m, c = divmod(j, 4)
                sp.dma_start(ring[:, s, :].rearrange("p (k n) -> p k n", n=D),
                             w_exp[m][e, :, 2 * c:2 * c + 2, :]).then_inc(ringIn[s], 16)

            def load_in(L, col):
                sp.dma_start(slot_k(L, 256), w_in[:, :, 256 * col:256 * col + 256]).then_inc(ringIn[L % NR], 16)

            for kind in ("f", "q", "i", "g"):
                for j in range(2):
                    load_in(W_CHUNK[kind][0] + j, W_CHUNK[kind][1] + j)
            sp.dma_start(s0, A["state_hgrn"][0].rearrange("b h k v -> k (b h) v")).then_inc(s0In, 16)
            for kind in ("cg", "vc", "bg"):
                for j in range(2):
                    load_in(W_CHUNK[kind][0] + j, W_CHUNK[kind][1] + j)
            sp.wait_ge(projMM, load_done(1))
            for m in range(3):
                for part in range(4):
                    sp.dma_start(biasRaw[32 * part:32 * part + 32, D * m:D * m + D], b_exp[m]).then_inc(biasIn, 16)
            for c in range(4):
                sp.wait_ge(projMM, load_done(L_WOUT + c - NR))
                sp.dma_start(slot_k(L_WOUT + c, D), w_out[:, 2 * c:2 * c + 2, :]).then_inc(ringIn[(L_WOUT + c) % NR], 16)
            for n in range(LPE * PER_BODY):
                L = L_EXP + n
                before = L - NR
                if before in (L_S0, L_S0 + 1):
                    sp.wait_ge(s0Out, 16)
                elif before in (L_BIAS, L_BIAS + 1):
                    sp.wait_ge(biasDone, 1)
                elif before < L_WOUT:
                    sp.wait_ge(projMM, load_done(before))
                elif before < L_EXP:
                    sp.wait_ge(woutMM, 3)
                else:
                    sp.wait_ge(wUsed, n - NR + 1 + START)
                load_expert(n // LPE, n % LPE, L % NR)

            def body(first, it):
                for n in range(LPE * PER_BODY):
                    sp.wait_ge(wUsed, (first + (n - NR + 1)) + it * (LPE * PER_BODY) + START)
                    load_expert(it * PER_BODY + n // LPE, n % LPE, (L_EXP + n) % NR)

            with sp.Fori(1, BODIES) as it:
                body(0, it)
            sp.wait_ge(flagDone, 1)
            with sp.Fori(1, ROUNDS) as r:
                more = sp.value_load(flag[0:1, bass.ds(r, 1)], min_val=0, max_val=1)
                with sp.If(more != 0):
                    with sp.Fori(0, BODIES) as it:
                        body(r * (LPE * E), it)
                    sp.nop()
                with sp.Else():
                    sp.nop()
            yp = A["y_prompt"][0].rearrange("(b p) d -> b p d", p=128)
            for b, (t0, n) in enumerate(TOK):
                sp.wait_ge(finDone, b + 1)
                dst = yp[b] if b < 2 else A["y_sample"].rearrange("s t d -> (s t) d")
                sp.dma_start(dst, yout[0:n, b, :]).then_inc(yOut, 16)
            sp.wait_ge(yOut, 48)
            sp.wait_ge(s0Out, 16)
            sp.wait_ge(stOut, 16)
            sp.wait_ge(tailOut, 32)

        @block.gpsimd
        def _(pool):
            rows = [("lb_logits", 8), ("conv_w", 12), ("conv_b", 4), ("gnorm_w", 4), ("norm_mix_w", 8), ("norm_ffn_w", 8)]
            at = 0
            for name, n in rows:
                pool.dma_start(parRows[at:at + n, :], A[name]).then_inc(parIn, 16)
                at += n
            pool.dma_start(histRows[0:16, :], A["state_conv"][0].rearrange("b w c -> (b w) c")).then_inc(histIn, 16)
            pool.dma_start(rw[:], A["router_w"][0].rearrange("(k p) e -> p k e", p=128)).then_inc(routerIn, 16)
            pool.dma_start(rb[:], A["router_b"][0].partition_broadcast(128)).then_inc(routerIn, 16)
            pool.wait_ge(mixDone, NH)
            pool.tensor_copy(tail[:, :, 0:2], u[:, :, NP:NP + 2])
            pool.tensor_copy(tail[:, :, 2:18].rearrange("p c (s w) -> p c s w", w=2),
                             u[:, :, NP + 2:].rearrange("p c (s w) -> p c s w", w=10)[:, :, :, 8:10]).then_inc(tailIn, 1)
            for h in range(NH):
                pool.wait_ge(projMM, len(UNITS))
                pool.wait_ge(oMM, NH)
                if h >= 2:
                    pool.wait_ge(stSMM, h - 1)
                if True:
                    pool.tensor_tensor(vSel[h % 2][0:64], v[0:64, 2, 128 * h:128 * h + 128].unsqueeze(1).broadcast_to([64, 8, 128]),
                                       seqMask[0:64, :].unsqueeze(2).broadcast_to([64, 8, 128]), ALU.mult).then_inc(vSelDone, 1)
                if h == 0:
                    pool.wait_ge(f8Out, 1)
                pool.tensor_tensor(s0v[:, :, h, :], s0v[:, :, h, :], f8[:, h, :].unsqueeze(2).broadcast_to([128, 8, 128]),
                                   ALU.mult).then_inc(s0Scaled, 1)
            pool.wait_ge(stSOut, NH)
            pool.dma_start(A["new_hgrn_sample"][0].rearrange("b h k v -> k (b h) v"), s0).then_inc(s0Out, 16)
            pool.wait_ge(biasIn, 16 * 12)
            pool.wait_ge(tailMM, 1)
            b3 = bias3.rearrange("p m d -> p (m d)")
            pool.tensor_copy(b3, biasRaw[:, 0:3 * D]).then_inc(biasStep, 1)
            pool.wait_ge(biasStep, 1)
            for n, lo in enumerate((64, 96)):
                pool.tensor_tensor(biasRaw[lo:128, 0:3 * D], biasRaw[lo:128, 0:3 * D], b3[lo:128], ALU.subtract).then_inc(biasStep, 1)
                pool.wait_ge(biasStep, 2 + 2 * n)
                pool.tensor_copy(b3[lo:128], biasRaw[lo:128, 0:3 * D]).then_inc(biasStep if n == 0 else biasDone, 1)
                if n == 0:
                    pool.wait_ge(biasStep, 3)
            pool.wait_ge(woutMM, 3)
            pool.dma_start(fnw, A["final_norm_w"].partition_broadcast(128)).then_inc(fnwIn, 16)

            def pick(value, par):
                pool.sem_inc(aloneP, 1)
                pool.tensor_copy(eh[:, par, :], expCol[:, value].broadcast_to([128, SLOTS])).then_inc(ehDone, 1)

            pool.wait_ge(biasDone, 1)
            pool.wait_ge(flagDone, 1)
            with pool.Fori(0, ROUNDS) as r:
                more = pool.value_load(flag[0:1, bass.ds(r, 1)], min_val=0, max_val=1)
                with pool.If(more != 0):
                    pool.wait_ge(wUsed, r * (LPE * E) + START)
                    pick(slice(0, 1), 0)
                    with pool.Fori(0, BODIES) as it:
                        for j in range(PER_BODY):
                            pool.wait_ge(wUsed, r * (LPE * E) + (it * (LPE * PER_BODY) + LPE * j) + START)
                            pick(bass.ds(it * PER_BODY + (j + 1), 1), (j + 1) % 2)
                    pool.nop()
                with pool.Else():
                    pool.nop()

        @block.scalar
        def _(act):
            credit(act, sigDone, xgOut, gtOut, hidTOut, yEvac)
            for b, (t0, n) in enumerate(TOK):
                src = A["x_prompt"][0, t0:t0 + n, :] if b < 2 else A["x_sample"].rearrange("s t d -> (s t) d")
                act.dma_start(x[0:n, b, :], src).then_inc(xIn[b], 16)
            act.dma_start(consts[:], A["consts"]).then_inc(constIn, 16)
            act.dma_start(maskIn, A["lev_mask"]).then_inc(constIn, 16)
            for b, (t0, n) in enumerate(TOK):
                act.wait_ge(xIn[b], 16)
                if b:
                    act.wait_ge(ssqDone, b)
                act.activation(junk[0:n], x[0:n, b, :], ACT.Square, accum_out=st[0:n, b:b + 1]).then_inc(ssqDone, 1)
            act.wait_ge(epsOut, 1)
            for b, (t0, n) in enumerate(TOK):
                act.wait_ge(ssqDone, b + 1)
                act.activation(st[0:n, 3 + b:4 + b], st[0:n, b:b + 1], ACT.Sqrt, bias=epsT[0:n, :], scale=1.0 / D)\
                   .then_inc(rootDone, 1)
            act.wait_ge(parOut, 2)
            act.activation(lbW[:, 1:3, :], lbW[:, 1:3, :], ACT.Exp).then_inc(expDone, 1)
            for item in SCHED:
                kind = item[0]
                if kind in ("f", "q", "i", "g", "cg"):
                    n = UIDX[item]
                    src = ps[:, n % 2, 0:NT]
                    act.wait_ge(projMM, n + 1)
                    out = unitOut[n % 2]
                if kind == "f":
                    h = item[1]
                    act.activation(fdec[:, h, :], src, ACT.Sigmoid)
                    act.activation(kS[:, h, :], src, ACT.Sigmoid, scale=-1.0).then_inc(out, 1)
                elif kind == "q":
                    act.activation(q[:, item[1], :], src, ACT.Copy).then_inc(out, 1)
                elif kind == "i":
                    _, c, b = item
                    act.wait_ge(maskOut, 1)
                    act.activation(v[0:TOK[b][1], b, 256 * c:256 * c + 256], ps[0:TOK[b][1], n % 2, 0:256], ACT.Copy)\
                       .then_inc(out, 1)
                elif kind == "g":
                    act.activation(g[:, item[1], :], src, ACT.Sigmoid).then_inc(gSig, 1)
                elif kind == "cg":
                    act.activation(cv[:, item[1], :], src, ACT.Copy).then_inc(out, 1)
                elif kind == "cross":
                    act.wait_ge(levMM, 2 * (NLEV + 1) + 1)
                    act.activation(sc[:, :, 256:384], ps[:, 6, :].rearrange("p (h t) -> p h t", h=4), ACT.Copy)\
                       .then_inc(crossOut, 1)
                elif kind == "o":
                    h = item[1]
                    act.wait_ge(oMM, h + 1)
                    act.activation(sc[:, h, 0:NT], ps[:, 2 + h, 0:NT], ACT.Square).then_inc(oSq, 1)
            for h in range(NH):
                act.wait_ge(ssMM, h + 1)
                act.activation(sc[:, h, 0:NT], ps[:, 6 + h % 2, 0:NT], ACT.Sqrt, bias=epsT[:], scale=1.0 / 128).then_inc(oRoot, 1)
            act.wait_ge(kTokMM, 1)
            act.activation(kTok[:, 0:8, :].rearrange("p n d -> p (n d)"), ps[:, 6:8, :].rearrange("p a n -> p (a n)"), ACT.Copy)
            act.activation(kTok[0:64, 8:12, :].rearrange("p n d -> p (n d)"), ps[0:64, 2, :], ACT.Copy).then_inc(kTokOut, 1)
            act.wait_ge(stPMM, 1)
            act.wait_ge(mixDone, NH)
            act.activation(stP.rearrange("p h d -> p (h d)"), ps[:, 3, :], ACT.Copy).then_inc(stPOut, 1)
            act.wait_ge(stPOut, 1)
            act.dma_start(A["new_hgrn_prompt"][0, 0].rearrange("h k v -> k h v"), stP).then_inc(stOut, 16)
            act.wait_ge(tailMM, 1)
            act.activation(tailT[0:18, :], ps[0:18, 2, :], ACT.Copy).then_inc(tailTOut, 1)
            act.wait_ge(tailTOut, 1)
            act.dma_start(A["new_conv_prompt"][0, 0], tailT[0:2, :]).then_inc(tailOut, 16)
            act.dma_start(A["new_conv_sample"][0].rearrange("b w c -> (b w) c"), tailT[2:18, :]).then_inc(tailOut, 16)

            for b, (t0, n) in enumerate(TOK):
                act.wait_ge(x2Done, b + 1)
                if b == 2:
                    act.wait_ge(h2Parts, 1)
                act.activation(h2f[0:n, b % 2, :], x[0:n, b, :], ACT.Square, accum_out=st[0:n, 9 + b:10 + b]).then_inc(ssq2Done, 1)
                act.wait_ge(ssq2Done, b + 1)
                act.activation(st[0:n, 12 + b:13 + b], st[0:n, 9 + b:10 + b], ACT.Sqrt, bias=epsT[0:n, :], scale=1.0 / D)\
                   .then_inc(root2Done, 1)
                act.wait_ge(x2TMM, b + 1)
                if b:
                    act.wait_ge(lgMM, b)
                act.activation(x2T[:, :, 0:n], ps[:, 6:8, :].rearrange("p a (k t) -> p (a k) t", t=128)[:, :, 0:n],
                               ACT.Copy).then_inc(x2TOut, 1)
                act.wait_ge(resid, 2 * b + 1)
                if b == 0:
                    act.wait_ge(stSMM, NH)
                act.activation(h2p[0:n, 0, b, :], h2f[0:n, b % 2, :], ACT.Copy).then_inc(partDone, 1)
                act.wait_ge(resid, 2 * b + 2)
                act.activation(h2p[0:n, 1, b, :], h2f[0:n, b % 2, :], ACT.Copy).then_inc(partDone, 1)
                act.wait_ge(mxDone, b + 1)
                act.activation(ex[0:n, b, :], lg[0:n, b, 0:4], ACT.Exp, accum_out=st[0:n, 18 + b:19 + b]).then_inc(exDone, 1)

            act.wait_ge(stOut, 16)
            act.wait_ge(tailOut, 32)
            act.wait_ge(flagDone, 1)
            with act.Fori(0, ROUNDS) as r:
                more = act.value_load(flag[0:1, bass.ds(r, 1)], min_val=0, max_val=1)
                with act.If(more != 0):
                    p0, e0 = r * (E + 1), r * E

                    def prefetch(m, e, par):
                        act.wait_ge(xgMM, m + 1 + START)
                        act.wait_ge(xgTMM, m + START)
                        act.activation(xgs, ps[:, 3, :], ACT.Copy).then_inc(xgOut, 1)
                        act.wait_ge(gtMM, m + 1 + START)
                        act.wait_ge(scatMM, e + START)
                        act.activation(GT[:, par, :], ps[:, 5, 0:NT], ACT.Copy).then_inc(gtOut, 1)

                    prefetch(p0, e0 * 3, 0)
                    with act.Fori(0, BODIES) as it:
                        for j in range(PER_BODY):
                            e = e0 + (it * PER_BODY + j)
                            m = p0 + (it * PER_BODY + (j + 1))
                            act.wait_ge(aDone, e + 1 + START)
                            act.wait_ge(hidDone, e + START)
                            act.activation(gs, ga, ACT.Sigmoid, scale=ALPHA).then_inc(sigDone, 1)
                            prefetch(m, e * 3, (j + 1) % 2)
                            act.wait_ge(hidTMM, e + 1 + START)
                            act.wait_ge(wUsed, e * LPE + START)
                            act.activation(hidT, ps[:, 4, :], ACT.Copy).then_inc(hidTOut, 1)
                            act.wait_ge(wUsed, e * LPE + LPE + START)
                            act.wait_ge(scatMM, e * 3 + START)
                            act.activation(ysb, ps[:, 2, :], ACT.Copy).then_inc(yEvac, 1)
                    act.nop()
                with act.Else():
                    act.nop()
            act.wait_ge(moeDone, 1)
            for b, (t0, n) in enumerate(TOK):
                if b:
                    act.wait_ge(finSq, b)
                act.activation(junk2[0:n], x[0:n, b, :], ACT.Square, accum_out=st[0:n, b:b + 1]).then_inc(finSq, 1)
                act.wait_ge(finSq, b + 1)
                act.activation(st[0:n, 3 + b:4 + b], st[0:n, b:b + 1], ACT.Sqrt, bias=epsT[0:n, :], scale=1.0 / D)\
                   .then_inc(finRoot, 1)

        @block.vector
        def _(dve):
            count = {}

            def did(ins, s=step):
                ins.then_inc(s, 1)
                count[s.name] = count.get(s.name, 0) + 1
                return s, count[s.name]

            def need(*done):
                for s, n in done:
                    dve.wait_ge(s, n)

            credit(dve, prep, aDone, uDone, tDone, hidDone, xgTOut, accDone)
            TT, TS, STT = dve.tensor_tensor, dve.tensor_scalar, dve.scalar_tensor_tensor
            did(dve.memset(epsT[:], EPS), epsOut)
            did(dve.memset(u[:, :, 0:2], 0.0))
            did(dve.memset(comb[:], 0.0))
            did(dve.memset(posm[:], 0.0))
            dve.wait_ge(constIn, 32)
            did(dve.tensor_copy(trib[:], tri))
            did(dve.tensor_copy(onesb[:], ones))
            did(dve.tensor_copy(levMask[:], maskIn), maskOut)
            for b, (t0, n) in enumerate(TOK):
                dve.wait_ge(rootDone, b + 1)
                need(did(dve.reciprocal(st[0:n, 6 + b:7 + b], st[0:n, 3 + b:4 + b])))
                TS(hs[0:n, b, :], x[0:n, b, :], st[0:n, 6 + b:7 + b], None, ALU.mult).then_inc(hsDone, 1)
            dve.wait_ge(parMM, 1)
            need(did(dve.tensor_copy(par[:], ps[:, 0, 0:44]), parOut))
            LB, CW, CB, GN, NM, NF = 0, 8, 20, 24, 28, 36
            did(dve.tensor_copy(u[:, :, NP + 2:].rearrange("p c (s w) -> p c s w", w=10)[:, :, :, 0:2],
                                ps[:, 1, 0:64].rearrange("p (c s w) -> p c s w", c=4, w=2)), histOut)
            need(did(TT(lbW[:, 0, :], par[:, LB:LB + 4], par[:, LB + 4:LB + 8], ALU.max)))
            did(TT(lbW[:, 1:3, :], par[:, LB:LB + 8].rearrange("p (a h) -> p a h", a=2),
                   lbW[:, 0, :].unsqueeze(1).broadcast_to([128, 2, 4]), ALU.subtract), parOut)
            for b, (t0, n) in enumerate(TOK):
                dve.wait_ge(xTMM, b + 1)
                TT(hT[:, :, t0:t0 + n], ps[:, 2 + 2 * b:4 + 2 * b, :].rearrange("p a (k t) -> p (a k) t", t=128)[:, :, 0:n],
                   par[:, NM:NM + 8].unsqueeze(2).broadcast_to([128, 8, n]), ALU.mult).then_inc(hTOut, 1)
            dve.wait_ge(expDone, 1)
            need(did(TT(lbW[:, 3, :], lbW[:, 1, :], lbW[:, 2, :], ALU.add)))
            need(did(dve.reciprocal(lbW[:, 4, :], lbW[:, 3, :])))
            need(did(TT(lb[:], lbW[:, 1, :], lbW[:, 4, :], ALU.mult)))
            need(did(TS(oml[:], lb[:], -1.0, 1.0, ALU.mult, ALU.add)))
            dve.wait_ge(routerIn, 32)
            did(TT(rw[:], rw[:], par[:, NF:NF + 8].unsqueeze(2).broadcast_to([128, 8, E]), ALU.mult))

            pairs = lambda ap, p: ap[:, 2 * p:2 * p + 2, :]
            fk, gk = {}, {}
            fp = {}
            convDone = {}
            for item in SCHED:
                kind = item[0]
                if kind in ("f", "g", "vc", "bg"):
                    n = UIDX[item]
                    src = ps[:, n % 2, :]
                if kind == "f":
                    h = item[1]
                    dve.wait_ge(unitOut[n % 2], n // 2 + 1)
                    did(TS(fdec[:, h, :], fdec[:, h, :], oml[:, h:h + 1], lb[:, h:h + 1], ALU.mult, ALU.add))
                    fk[h] = did(TS(kS[:, h, :], kS[:, h, :], oml[:, h:h + 1], None, ALU.mult), kScaled)
                elif kind == "g":
                    h = item[1]
                    dve.wait_ge(gSig, h + 1)
                    gk[h] = did(STT(g[:, h, :], src[:, 0:NT], par[:, GN + h:GN + h + 1], g[:, h, :], ALU.mult, ALU.mult), unitOut[n % 2])
                elif kind == "vc":
                    c = item[1]
                    m = UIDX[("cg", c)]
                    dve.wait_ge(unitOut[m % 2], m // 2 + 1)
                    dve.wait_ge(projMM, n + 1)
                    us = u[:, c, NP + 2:].rearrange("p (s w) -> p s w", w=10)
                    did(TT(u[:, c, 2:NP + 2], src[:, 0:NP], cv[:, c, 0:NP], ALU.mult))
                    TT(us[:, :, 2:10], src[:, NP:NT].rearrange("p (s w) -> p s w", w=8),
                       cv[:, c, NP:NT].rearrange("p (s w) -> p s w", w=8), ALU.mult).then_inc(unitOut[n % 2], 1)
                    dve.wait_ge(unitOut[n % 2], n // 2 + 1)
                    cp, cs = cv[:, c, 0:NP], cv[:, c, NP:NT].rearrange("p (s w) -> p s w", w=8)
                    w = lambda j: par[:, CW + 4 * j + c:CW + 4 * j + c + 1]
                    did(TS(cp, u[:, c, 0:NP], w(0), par[:, CB + c:CB + c + 1], ALU.mult, ALU.add))
                    done = did(TS(cs, us[:, :, 0:8], w(0), par[:, CB + c:CB + c + 1], ALU.mult, ALU.add))
                    for j in (1, 2):
                        need(done)
                        did(STT(cp, u[:, c, j:NP + j], w(j), cp, ALU.mult, ALU.add))
                        done = did(STT(cs, us[:, :, j:8 + j], w(j), cs, ALU.mult, ALU.add))
                    convDone[c] = done
                elif kind == "bg":
                    c = item[1]
                    dve.wait_ge(projMM, n + 1)
                    need(convDone[c])
                    TT(mixT[:, c, :], src[:, 0:NT], cv[:, c, :], ALU.mult).then_inc(unitOut[n % 2], 1)
                elif kind == "lev":
                    _, l, p = item
                    dve.wait_ge(levMM, 2 * l + p + 1)
                    pb = ps[:, 2 + 2 * p:4 + 2 * p, :]
                    tiles = pb[:, :, 0:256].rearrange("p h (b t) -> p h b t", b=2)
                    smp = pb[0:64, :, 256:320]
                    outT = pairs(sc, p)[:, :, 0:256].rearrange("p h (b t) -> p h b t", b=2)
                    outS = pairs(sc, p)[0:64, :, 384:448]
                    if l == 0:
                        did(TT(outT, tiles, ident.unsqueeze(1).unsqueeze(1).broadcast_to([128, 2, 2, 128]), ALU.mult))
                        need(did(TT(outS, smp, ident[0:64, 0:64].unsqueeze(1).broadcast_to([64, 2, 64]), ALU.mult)))
                        mq = [UIDX[("q", 2 * p)], UIDX[("q", 2 * p + 1)]]
                        need(fk[2 * p + 1])
                        for m in mq:
                            dve.wait_ge(unitOut[m % 2], m // 2 + 1)
                        fp[p] = did(TT(pairs(qP, p), pairs(q, p), pairs(fdec, p), ALU.mult), levOut)
                    else:
                        size = 1 << (l - 1)
                        for hh in range(2):
                            m_ = levMask[:, l - 1, :].unsqueeze(1).broadcast_to([128, 2, 128])
                            last = did(dve.copy_predicated(outT[:, hh], m_, tiles[:, hh]))
                        if l <= 3:
                            m_ = levMask[0:64, l - 1, 0:64].unsqueeze(1).broadcast_to([64, 2, 64])
                            last = did(dve.copy_predicated(outS, m_, smp))
                        need(last, fp[p])
                        cols = NT if size <= 4 else NP
                        blk = lambda ap: pairs(ap, p)[:, :, 0:cols].rearrange("p h (b two t) -> p h b two t", two=2, t=size)
                        nb = cols // (2 * size)
                        fv, qv, kv = blk(fdec), blk(qP), blk(kS)
                        shape = [128, 2, nb, size]
                        did(TT(qv[:, :, :, 1, :], qv[:, :, :, 1, :], fv[:, :, :, 0, size - 1:size].broadcast_to(shape), ALU.mult))
                        need(did(TT(kv[:, :, :, 0, :], kv[:, :, :, 0, :], fv[:, :, :, 1, size - 1:size].broadcast_to(shape), ALU.mult)))
                        fp[p] = did(TT(fv[:, :, :, 1, size - 1], fv[:, :, :, 1, size - 1], fv[:, :, :, 0, size - 1], ALU.mult), levOut)
                        if l == 3 and p == 1:
                            need(fp[0], fp[1])
                            did(dve.tensor_copy(f8[:], fdec[:, :, NP + 7:NT:8]), f8Out)
                elif kind == "cross":
                    dve.wait_ge(levMM, 2 * (NLEV + 1) + 1)
                    need(fp[0], fp[1])
                    did(TT(kS[:, :, 0:128], kS[:, :, 0:128], fdec[:, :, 255:256].broadcast_to([128, 4, 128]), ALU.mult), levOut)
            for h in range(NH):
                dve.wait_ge(oRoot, h + 1)
                need(gk[h], did(dve.reciprocal(sc[:, h, 0:NT], sc[:, h, 0:NT])))
                need(did(TT(g[:, h, :], g[:, h, :], sc[:, h, 0:NT], ALU.mult)))
                TT(mixT[:, NH + h, :], ps[:, 2 + h, 0:NT], g[:, h, :], ALU.mult).then_inc(mixDone, 1)
            for h in range(NH):
                dve.wait_ge(stSMM, h + 1)
                dve.wait_ge(s0Scaled, h + 1)
                TT(s0v[:, :, h, :], s0v[:, :, h, :], ps[:, 4:6, :].rearrange("p a (b d) -> p (a b) d", d=128), ALU.add)\
                    .then_inc(stSOut, 1)

            WB = [0, 2, 4]
            for b, (t0, n) in enumerate(TOK):
                dve.wait_ge(woutMM, b + 1)
                if b < 2:
                    TT(x[0:n, b, :], x[0:n, b, :], ps[0:n, WB[b]:WB[b] + 2, :].rearrange("p a n -> p (a n)"), ALU.add)\
                        .then_inc(x2Done, 1)
                else:
                    did(TT(x[0:n, b, 0:512], x[0:n, b, 0:512], ps[0:n, WB[b], :], ALU.add))
                    TT(x[0:n, b, 512:1024], x[0:n, b, 512:1024], ps[64:64 + n, WB[b], :], ALU.add).then_inc(x2Done, 1)
                rstd = st[0:n, 15 + b:16 + b]
                dve.wait_ge(root2Done, b + 1)
                need(did(dve.reciprocal(rstd, st[0:n, 12 + b:13 + b])))
                hf = h2f[0:n, b % 2, :]
                if b == 2:
                    dve.wait_ge(h2Parts, 1)
                dve.wait_ge(x2Done, b + 1)
                TS(hf, x[0:n, b, :], rstd, None, ALU.mult).then_inc(resid, 1)
                dve.wait_ge(partDone, 2 * b + 1)
                TT(hf, hf, h2p[0:n, 0, b, :], ALU.subtract).then_inc(resid, 1)
                dve.wait_ge(lgMM, b + 1)
                need(did(STT(lg[0:n, b, :], ps[0:n, 5, E * b:E * b + E], rstd, rb[0:n, :], ALU.mult, ALU.add)))
                need(did(dve.max(mx[0:n, b, :], lg[0:n, b, :])))
                need(did(dve.max_index(mi[0:n, b, :], mx[0:n, b, :], lg[0:n, b, :])))
                did(TS(lg[0:n, b, 0:4], mx[0:n, b, 0:4], mx[0:n, b, 0:1], None, ALU.subtract), mxDone)
                last = did(dve.tensor_copy(mif[0:n, b, :], mi[0:n, b, :]))
                dve.wait_ge(partDone, 2 * b + 2)
                did(TT(h2p[0:n, 2, b, :], hf, h2p[0:n, 1, b, :], ALU.subtract), h2Parts)
                dve.wait_ge(exDone, b + 1)
                need(last, did(dve.reciprocal(st[0:n, 21 + b:22 + b], st[0:n, 18 + b:19 + b])))
                need(did(TS(ex[0:n, b, :], ex[0:n, b, :], st[0:n, 21 + b:22 + b], None, ALU.mult)))
                for k in range(TOPK):
                    dst = comb[0:n, b, 0:E] if k == 0 else oh[0:n, 0, :]
                    done = did(TS(dst, expId[0:n, :], mif[0:n, b, k:k + 1], ex[0:n, b, k:k + 1], ALU.is_equal, ALU.mult))
                    need(done)
                    if k:
                        need(did(TT(comb[0:n, b, 0:E], comb[0:n, b, 0:E], oh[0:n, 0, :], ALU.add)))
                TS(sel[0:n, b, :], comb[0:n, b, 0:E], 0.0, None, ALU.is_gt).then_inc(selDone, 1)
            dve.wait_ge(selDone, 3)
            dve.wait_ge(posMM, 1)
            for b, (t0, n) in enumerate(TOK):
                need(did(STT(posm[0:n, b, 0:E], ps[0:n, 5, 128 + E * b:128 + E * b + E], 1.0, sel[0:n, b, :], ALU.add, ALU.mult)))
            did(TS(posm[:], posm[:], float(SLOTS), None, ALU.add), posOut)
            need(did(dve.tensor_reduce(cmax[0:1, :], ps[0:1, 5, 256:256 + E], AX.X, ALU.max)))
            need(did(TS(flag[0:1, :], roundStart[0:1, :], cmax[0:1, 0:1], None, ALU.is_lt)))
            did(dve.memset(flag[0:1, 0:1], 1), flagDone)
            dve.wait_ge(flagDone, 1)
            dve.wait_ge(posOut, 1)
            dve.wait_ge(stOut, 16)
            dve.wait_ge(tailOut, 32)

            with dve.Fori(0, ROUNDS) as r:
                more = dve.value_load(flag[0:1, bass.ds(r, 1)], min_val=0, max_val=1)
                with dve.If(more != 0):
                    p0, e0 = r * (E + 1), r * E

                    def prepare(m, col):
                        dve.wait_ge(xgMM, m + START)
                        dve.wait_ge(gtMM, m + START)
                        for b, (t0, n) in enumerate(TOK):
                            TS(P[0:n, b, :], iota2[0:n, 0:SLOTS], posm[0:n, b, col], None, ALU.is_equal)
                            ins = TS(G[0:n, b, :], iota2[0:n, :], posm[0:n, b, col], comb[0:n, b, col], ALU.is_equal, ALU.mult)
                        ins.then_inc(prep, 1)

                    def gathered(m):
                        dve.wait_ge(xgTMM, m + 1 + START)
                        TT(xgT.rearrange("p (c a s) -> p c a s", c=4, a=2),
                           ps[:, 3, :].rearrange("p (c a s) -> p c a s", c=4, a=2),
                           par[:, NF:NF + 8].rearrange("p (a c) -> p c a", a=2).unsqueeze(3).broadcast_to([128, 4, 2, SLOTS]),
                           ALU.mult).then_inc(xgTOut, 1)

                    TS(posm[:], posm[:], -float(SLOTS), None, ALU.add).then_inc(posShift, 1)
                    dve.wait_ge(posShift, r + 1)
                    prepare(p0, slice(0, 1))
                    gathered(p0)
                    with dve.Fori(0, BODIES) as it:
                        for j in range(PER_BODY):
                            e = e0 + (it * PER_BODY + j)
                            m = p0 + (it * PER_BODY + (j + 1))
                            prepare(m, bass.ds(it * PER_BODY + (j + 1), 1))
                            dve.wait_ge(wUsed, e * LPE + 4 + START)
                            TS(ga, ps[:, 0, :], LIMIT, None, ALU.min).then_inc(aDone, 1)
                            dve.wait_ge(wUsed, e * LPE + 8 + START)
                            TS(gu, ps[:, 1, :], LIMIT, -LIMIT, ALU.min, ALU.max).then_inc(uDone, 1)
                            dve.wait_ge(aDone, e + 1 + START)
                            dve.wait_ge(uDone, e + 1 + START)
                            STT(gt, gu, 1.0, ga, ALU.add, ALU.mult).then_inc(tDone, 1)
                            dve.wait_ge(sigDone, e + 1 + START)
                            dve.wait_ge(tDone, e + 1 + START)
                            dve.wait_ge(hidTMM, e + START)
                            TT(hid, gt, gs, ALU.mult).then_inc(hidDone, 1)
                            gathered(m)
                            for b, (t0, n) in enumerate(TOK):
                                dve.wait_ge(scatMM, e * 3 + (b + 1) + START)
                                dve.wait_ge(accDone, e * 3 + b + START)
                                TT(x[0:n, b, :], x[0:n, b, :], ps[0:n, 6:8, :].rearrange("p a n -> p (a n)"), ALU.add)\
                                    .then_inc(accDone, 1)
                    dve.wait_ge(accDone, (r + 1) * (3 * E) + START)
                    dve.wait_ge(xgTOut, (r + 1) * (E + 1) + START)
                    dve.sem_inc(aloneV, 1)
                with dve.Else():
                    dve.nop()
            dve.nop().then_inc(moeDone, 1)
            dve.wait_ge(fnwIn, 16)
            for b, (t0, n) in enumerate(TOK):
                dve.wait_ge(finRoot, b + 1)
                need(did(dve.reciprocal(st[0:n, 6 + b:7 + b], st[0:n, 3 + b:4 + b])))
                STT(yout[0:n, b, :], x[0:n, b, :], st[0:n, 6 + b:7 + b], fnw[0:n], ALU.mult, ALU.mult).then_inc(finDone, 1)

        @block.tensor
        def _(pe):
            MM, TR = pe.matmul, pe.transpose
            credit(pe, wUsed, xgMM, gtMM, xgTMM, hidTMM, scatMM)
            pe.wait_ge(parIn, 16 * 6)
            pe.wait_ge(histIn, 16)
            pe.wait_ge(constIn, 32)
            for c in range(4):
                TR(ps[:, 1, 16 * c:16 * c + 16], histRows[0:16, 128 * c:128 * c + 128], ident[0:16, 0:16])
            TR(ps[:, 0, 0:44], parRows[:], ident[0:44, 0:44]).then_inc(parMM, 1)
            for b, (t0, n) in enumerate(TOK):
                pe.wait_ge(hsDone, b + 1)
                for k in range(KT):
                    ins = TR(ps[:, 2 + 2 * b + k // 4, 128 * (k % 4):128 * (k % 4) + n], hs[0:n, b, 128 * k:128 * k + 128],
                             ident[0:n, 0:n])
                ins.then_inc(xTMM, 1)
            pe.wait_ge(hTOut, 3)
            pe.wait_ge(histOut, 1)
            for item in SCHED:
                kind = item[0]
                if item in UIDX:
                    n = UIDX[item]
                    l0 = W_CHUNK[kind][0]
                    if n >= 2:
                        pe.wait_ge(unitOut[n % 2], n // 2)
                    if kind == "i":
                        _, c, b = item
                        t0, nt = TOK[b]
                        L = l0 + c
                        pe.wait_ge(ringIn[L % NR], ring_value(L))
                        for k in range(KT):
                            ins = MM(ps[0:nt, n % 2, 0:256], hT[:, k, t0:t0 + nt], slot_k(L, 256)[:, k, :],
                                     start=(k == 0), stop=(k == KT - 1))
                    else:
                        L, half = l0 + item[1] // 2, item[1] % 2
                        pe.wait_ge(ringIn[L % NR], ring_value(L))
                        for k in range(KT):
                            ins = MM(ps[:, n % 2, 0:NT], slot_k(L, 256)[:, k, 128 * half:128 * half + 128], hT[:, k, :],
                                     start=(k == 0), stop=(k == KT - 1))
                    ins.then_inc(projMM, 1)
                elif kind == "lev":
                    _, l, p = item
                    if l == 0:
                        for kk in ("f", "q"):
                            for h in (2 * p, 2 * p + 1):
                                m = UIDX[(kk, h)]
                                pe.wait_ge(unitOut[m % 2], m // 2 + 1)
                        pe.wait_ge(kScaled, 2 * p + 2)
                    else:
                        pe.wait_ge(levOut, 2 * (l - 1) + p + 1)
                    src = q if l == 0 else qP
                    for hh in range(2):
                        h = 2 * p + hh
                        for b in range(2):
                            ins = MM(ps[:, 2 + h, 128 * b:128 * b + 128], kS[:, h, 128 * b:128 * b + 128],
                                     src[:, h, 128 * b:128 * b + 128], start=True, stop=True)
                        if l <= 3:
                            ins = MM(ps[0:64, 2 + h, NP:NT], kS[:, h, NP:NT], src[:, h, NP:NT], start=True, stop=True)
                    ins.then_inc(levMM, 1)
                elif kind == "cross":
                    pe.wait_ge(levOut, 2 * (NLEV + 1))
                    for h in range(NH):
                        ins = MM(ps[:, 6, 128 * h:128 * h + 128], kS[:, h, 0:128], qP[:, h, 128:256], start=True, stop=True)
                    ins.then_inc(levMM, 1)
                elif kind == "o":
                    h = item[1]
                    if h == 0:
                        pe.wait_ge(crossOut, 1)
                        pe.wait_ge(s0In, 16)
                    o = ps[:, 2 + h, :]
                    hv = slice(128 * h, 128 * h + 128)
                    MM(o[:, 0:128], v[:, 0, hv], sc[:, h, 0:128], start=True, stop=False, skip_group_check=True)
                    MM(o[:, 128:256], v[:, 0, hv], sc[:, h, 256:384], start=False, stop=False, skip_group_check=True)
                    MM(o[:, 128:256], v[:, 1, hv], sc[:, h, 128:256], start=False, stop=False, skip_group_check=True)
                    MM(o[:, NP:NT], v[0:64, 2, hv], sc[0:64, h, 384:448], start=False, stop=False, skip_group_check=True)
                    for s in range(NSEQ):
                        t = NP + LS * s
                        ins = MM(o[:, t:t + LS], s0v[:, s, h, :], qP[:, h, t:t + LS], start=False, stop=True, skip_group_check=True)
                    ins.then_inc(oMM, 1)
            for h in range(NH):
                pe.wait_ge(oSq, h + 1)
                if h >= 2:
                    pe.wait_ge(oRoot, h - 1)
                MM(ps[:, 6 + h % 2, 0:NT], ones, sc[:, h, 0:NT], start=True, stop=True).then_inc(ssMM, 1)
            pe.wait_ge(oRoot, NH)
            pe.wait_ge(levOut, 2 * (NLEV + 1) + 1)
            pe.wait_ge(mixDone, 1)
            for h in range(NH):
                for b in range(2):
                    TR(ps[:, 6 + h // 2, 256 * (h % 2) + 128 * b:256 * (h % 2) + 128 * b + 128], kS[:, h, 128 * b:128 * b + 128], ident)
            for h in range(NH):
                ins = TR(ps[0:64, 2, 128 * h:128 * h + 128], kS[:, h, NP:NT], ident)
            ins.then_inc(kTokMM, 1)
            pe.wait_ge(kTokOut, 1)
            pe.wait_ge(mixDone, 2)
            for h in range(NH):
                for b in range(2):
                    ins = MM(ps[:, 3, 128 * h:128 * h + 128], kTok[:, 2 * h + b, :], v[:, b, 128 * h:128 * h + 128],
                             start=(b == 0), stop=(b == 1))
            ins.then_inc(stPMM, 1)

            def sample_state(h):
                pe.wait_ge(vSelDone, h + 1)
                if h:
                    pe.wait_ge(stSOut, h)
                for a in range(2):
                    ins = MM(ps[:, 4 + a, :], kTok[0:64, 8 + h, :], vSel[h % 2][0:64, 4 * a:4 * a + 4, :].rearrange("p b d -> p (b d)"),
                             start=True, stop=True)
                ins.then_inc(stSMM, 1)

            def tails():
                pe.wait_ge(tailIn, 1)
                for c in range(4):
                    ins = TR(ps[0:18, 2, 128 * c:128 * c + 128], tail[:, c, :], ident)
                ins.then_inc(tailMM, 1)

            def wout(b):
                t0, n = TOK[b]
                for k in range(KT):
                    L = L_WOUT + k // 2
                    w = slot_k(L, D)[:, k % 2, :]
                    if b == 0 and k % 2 == 0:
                        pe.wait_ge(ringIn[L % NR], ring_value(L))
                    for half in range(2):
                        dst = ps[0:n, 2 * b + half, :] if b < 2 else ps[64 * half:64 * half + 64, 4, :]
                        ins = MM(dst, mixT[:, k, t0:t0 + n], w[:, 512 * half:512 * half + 512], start=(k == 0), stop=(k == KT - 1))
                ins.then_inc(woutMM, 1)

            def logits(b):
                t0, n = TOK[b]
                pe.wait_ge(x2Done, b + 1)
                if b:
                    pe.wait_ge(x2TOut, b)
                for k in range(KT):
                    ins = TR(ps[:, 6 + k // 4, 128 * (k % 4):128 * (k % 4) + n], x[0:n, b, 128 * k:128 * k + 128], ident[0:n, 0:n])
                ins.then_inc(x2TMM, 1)
                pe.wait_ge(x2TOut, b + 1)
                for k in range(KT):
                    ins = MM(ps[0:n, 5, E * b:E * b + E], x2T[:, k, 0:n], rw[:, k, :], start=(k == 0), stop=(k == KT - 1))
                ins.then_inc(lgMM, 1)

            pe.wait_ge(unitOut[0], len(UNITS) // 2)
            pe.wait_ge(unitOut[1], len(UNITS) // 2)
            pe.wait_ge(mixDone, NH)
            wout(0)
            tails()
            sample_state(0)
            sample_state(1)
            pe.wait_ge(tailTOut, 1)
            pe.wait_ge(stPOut, 1)
            wout(1)
            sample_state(2)
            sample_state(3)
            logits(0)
            pe.wait_ge(stSOut, NH)
            wout(2)
            logits(1)
            logits(2)
            pe.wait_ge(selDone, 3)
            for b, (t0, n) in enumerate(TOK):
                for a in range(b):
                    MM(ps[0:n, 5, 128 + E * b:128 + E * b + E], onesb[:, 0:n], sel[:, a, :], start=(a == 0), stop=False)
                MM(ps[0:n, 5, 128 + E * b:128 + E * b + E], trib[0:n, 0:n], sel[0:n, b, :], start=(b == 0), stop=True)
            for b, (t0, n) in enumerate(TOK):
                ins = MM(ps[:, 5, 256:256 + E], onesb[0:n, :], sel[0:n, b, :], start=(b == 0), stop=(b == 2))
            ins.then_inc(posMM, 1)
            pe.wait_ge(h2Parts, 3)
            pe.wait_ge(biasDone, 1)
            pe.wait_ge(flagDone, 1)

            with pe.Fori(0, ROUNDS) as r:
                more = pe.value_load(flag[0:1, bass.ds(r, 1)], min_val=0, max_val=1)
                with pe.If(more != 0):
                    p0, e0 = r * (E + 1), r * E

                    def gather(m):
                        pe.wait_ge(prep, m + 1 + START)
                        pe.wait_ge(xgTOut, m + START)
                        for b, (t0, n) in enumerate(TOK):
                            for part in range(3):
                                for half in range(2):
                                    ins = MM(ps[64 * half:64 * half + 64, 3, :], P[0:n, b, :],
                                             h2p[0:n, part, b, 512 * half:512 * half + 512],
                                             start=(b == 0 and part == 0), stop=(b == 2 and part == 2))
                        ins.then_inc(xgMM, 1)
                        pe.wait_ge(gtOut, m + START)
                        for b, (t0, n) in enumerate(TOK):
                            ins = TR(ps[:, 5, t0:t0 + n], G[0:n, b, :], ident[0:n, 0:n])
                        ins.then_inc(gtMM, 1)

                    def turn(m):
                        pe.wait_ge(xgOut, m + 1 + START)
                        for c in range(4):
                            ins = TR(ps[:, 3, 128 * c:128 * c + 128], xgs[:, 128 * c:128 * c + 128], ident)
                        ins.then_inc(xgTMM, 1)

                    def product(mat, bank, lhs, e, it, j):
                        for half in range(2):
                            MM(ps[64 * half:64 * half + 64, bank, :], eh[:, j % 2, :], bias3[:, mat, 512 * half:512 * half + 512],
                               start=True, stop=False)
                        for k in range(KT):
                            n = LPE * j + 4 * mat + k // 2
                            s = (L_EXP + n) % NR
                            if k % 2 == 0:
                                pe.wait_ge(ringIn[s], (r * BODIES + it) * (16 * PER_BODY * LPE // NR) + ring_value(L_EXP + n))
                            w = ring[:, s, D * (k % 2):D * (k % 2) + D]
                            for half in range(2):
                                ins = MM(ps[64 * half:64 * half + 64, bank, :], lhs(k), w[:, 512 * half:512 * half + 512],
                                         start=False, stop=(k == KT - 1))
                            if k % 2:
                                ins.then_inc(wUsed, 1)

                    half_c = lambda ap: (lambda k: ap[:, 128 * (k % 4) + 64 * (k // 4):128 * (k % 4) + 64 * (k // 4) + 64])
                    gather(p0)
                    turn(p0)
                    with pe.Fori(0, BODIES) as it:
                        for j in range(PER_BODY):
                            e = e0 + (it * PER_BODY + j)
                            m = p0 + (it * PER_BODY + (j + 1))
                            pe.wait_ge(ehDone, m)
                            pe.wait_ge(xgTOut, m + START)
                            pe.wait_ge(aDone, e + START)
                            product(0, 0, half_c(xgT), e, it, j)
                            pe.wait_ge(uDone, e + START)
                            product(1, 1, half_c(xgT), e, it, j)
                            gather(m)
                            turn(m)
                            pe.wait_ge(hidDone, e + 1 + START)
                            pe.wait_ge(hidTOut, e + START)
                            for c in range(4):
                                ins = TR(ps[:, 4, 128 * c:128 * c + 128], hid[:, 128 * c:128 * c + 128], ident)
                            ins.then_inc(hidTMM, 1)
                            pe.wait_ge(hidTOut, e + 1 + START)
                            pe.wait_ge(yEvac, e + START)
                            product(2, 2, half_c(hidT), e, it, j)
                            pe.wait_ge(yEvac, e + 1 + START)
                            pe.wait_ge(gtOut, m + START)
                            for b, (t0, n) in enumerate(TOK):
                                pe.wait_ge(accDone, e * 3 + b + START)
                                if n == 64:
                                    pe.sem_inc(aloneT, 1)
                                for half in range(2):
                                    ins = MM(ps[0:n, 6 + half, :], GT[64 * half:64 * half + 64, j % 2, t0:t0 + n],
                                             ysb[64 * half:64 * half + 64, :], start=True, stop=True)
                                ins.then_inc(scatMM, 1)
                    pe.nop()
                with pe.Else():
                    pe.nop()


_IN = ["x_prompt", "x_sample", "state_conv", "state_hgrn", "w_in", "w_out", "router_w", "router_b", "w_gate", "b_gate",
       "w_up", "b_up", "w_down", "b_down", "final_norm_w"]
_ROWS = ["lb_logits", "conv_w", "conv_b", "gnorm_w", "norm_mix_w", "norm_ffn_w"]
_OUT = [("y_prompt", (1, 256, 1024)), ("y_sample", (8, 8, 1024)), ("new_conv_prompt", (1, 1, 2, 512)),
        ("new_hgrn_prompt", (1, 1, 4, 128, 128)), ("new_conv_sample", (1, 8, 2, 512)),
        ("new_hgrn_sample", (1, 8, 4, 128, 128))]


def _constants():
    import numpy as np
    p = np.arange(128)
    slots = np.tile(np.arange(1, 65), 2)
    pick = (p[:, None] % 32 == np.arange(34)[None]) & (p[:, None] // 32 != 1)
    parts = [np.eye(128), p[:, None] < p[None], np.ones((128, 128)), np.broadcast_to(slots, (128, 128)), pick,
             np.broadcast_to(64 * np.arange(8), (128, 8)), p[:, None] // 8 == np.arange(8)[None],
             np.broadcast_to(np.arange(32), (128, 32))]
    consts = np.ascontiguousarray(np.concatenate([a.astype(np.float32) for a in parts], axis=1))
    s, t = p[:, None], p[None]
    lev = [(s // (2 * n) == t // (2 * n)) & (s // n % 2 == 0) & (t // n % 2 == 1) for n in (1, 2, 4, 8, 16, 32, 64)]
    return consts, np.ascontiguousarray(np.stack(lev, axis=1).astype(np.float32))


def kernel(**inputs):
    import numpy as np
    import concourse.bacc as bacc
    from concourse.bass_utils import run_bass_kernel_spmd

    nc = bacc.Bacc("TRN2", target_bir_lowering=False, num_devices=1)
    arrays = {n: np.ascontiguousarray(inputs[n]) for n in _IN}
    for n in _ROWS:
        arrays[n] = np.ascontiguousarray(inputs[n]).reshape(-1, 128)
    arrays["consts"], arrays["lev_mask"] = _constants()
    aps = {n: nc.dram_tensor("in_" + n, a.shape, mybir.dt.from_np(a.dtype), kind="ExternalInput").ap()
           for n, a in arrays.items()}
    for n, shape in _OUT:
        aps[n] = nc.dram_tensor(n, shape, mybir.dt.float32, kind="ExternalOutput").ap()
    hybrid_shortconv_hgrn2_moe_step(nc, aps)
    r = run_bass_kernel_spmd(nc, [{"in_" + n: a for n, a in arrays.items()}], core_ids=[0])
    return tuple(r.results[0][n] for n, _ in _OUT)
```

```python
import concourse.bass as bass
from concourse import mybir
from contextlib import ExitStack


def hybrid_shortconv_hgrn2_moe_step(nc, A):
    f32, bf16, u8 = mybir.dt.float32, mybir.dt.bfloat16, mybir.dt.uint8
    i32, u32 = mybir.dt.int32, mybir.dt.uint32
    ALU, ACT, AX = mybir.AluOpType, mybir.ActivationFunctionType, mybir.AxisListType

    D = 1024
    KT = D // 128
    NP, NSEQ, LS = 256, 8, 8
    NT = NP + NSEQ * LS
    TOK = [(0, 128), (128, 128), (256, 64)]
    NH = 4
    E = 32
    SLOTS = 64
    ROUNDS = NT // SLOTS
    TOPK = 4
    LIMIT, ALPHA, EPS = 7.0, 1.702, 1e-6
    NLEV = 7

    NR = 16
    W_CHUNK = {"f": (0, 8), "q": (2, 6), "i": (4, 10), "g": (6, 12), "cg": (10, 2), "vc": (12, 4), "bg": (14, 0)}
    L_S0, L_BIAS, L_WOUT, L_EXP = 8, 16, 18, 22
    LPE = 12
    PER_BODY = 4
    BODIES = E // PER_BODY
    NO_RING_SEM = {0, 1, 8, 9}

    def ring_value(L):
        special = (L_S0, L_S0 + 1, L_BIAS, L_BIAS + 1)
        return 16 * sum(1 for q in range(L % NR, L + 1, NR) if q not in special)

    UNITS = ([("f", h) for h in range(NH)] + [("q", h) for h in range(NH)]
             + [("i", c, b) for c in range(2) for b in range(3)] + [("g", h) for h in range(NH)]
             + [("cg", c) for c in range(NH)] + [("vc", c) for c in range(NH)] + [("bg", c) for c in range(NH)])
    UIDX = {u: n for n, u in enumerate(UNITS)}
    STEPS = ([("lev", l, p) for l in range(NLEV + 1) for p in range(2)] + [("cross",)] + [("o", h) for h in range(NH)]
             + [("ss", h) for h in range(NH)] + [("ktok",), ("stp",)] + [("sts", h) for h in range(NH)])
    SCHED = []
    left = list(STEPS)
    for n, u in enumerate(UNITS):
        SCHED.append(u)
        for _ in range(0 if n < 8 else 1 + n % 2):
            if left:
                SCHED.append(left.pop(0))
    SCHED += left

    def load_done(L):
        for kind, (l0, _) in W_CHUNK.items():
            if l0 <= L < l0 + 2:
                return 1 + (UIDX[(kind, L - l0, 2)] if kind == "i" else UIDX[(kind, 2 * (L - l0) + 1)])

    ctx = ExitStack()
    with ctx:
        def sb(name, shape, dt=f32):
            return ctx.enter_context(nc.sbuf_tensor(name, shape, dt))

        def sem(name):
            return ctx.enter_context(nc.semaphore(name))

        ring = sb("ring", [128, NR, 2048])
        x = sb("x", [128, 3, D])
        R1 = sb("R1", [128, 5120])
        R2 = sb("R2", [128, 2560])
        R3 = sb("R3", [128, 4608])
        R4 = sb("R4", [128, 2632])

        def view(region, at, pattern=None, **kw):
            n = 1
            for v in kw.pop("shape"):
                n *= v
            ap = region[:, at:at + n]
            return ap.rearrange(pattern, **kw) if pattern else ap

        hT = view(R1, 0, "p (k t) -> p k t", shape=(8, NT), k=8)
        qP = view(R1, 2560, "p (h t) -> p h t", shape=(4, NT), h=4)
        kS = view(R1, 3840, "p (h t) -> p h t", shape=(4, NT), h=4)
        vSel = [view(R1, at, "p (b d) -> p b d", shape=(8, 128), b=8) for at in (2560, 3584)]
        h2p = R1[:, 0:4608].bitcast(bf16).rearrange("p (s b d) -> p s b d", s=3, b=3)
        yout = view(R1, 0, "p (b d) -> p b d", shape=(3, D), b=3)
        junk2 = view(R1, 3072, shape=(D,))
        mixT = view(R2, 0, "p (k t) -> p k t", shape=(8, NT), k=8)
        fdec = view(R2, 0, "p (h t) -> p h t", shape=(4, NT), h=4)
        q = view(R2, 1280, "p (h t) -> p h t", shape=(4, NT), h=4)
        fnw = view(R2, 0, shape=(D,))
        g = view(R3, 0, "p (h t) -> p h t", shape=(4, NT), h=4)
        sc = view(R3, 1280, "p (h t) -> p h t", shape=(4, 448), h=4)
        v = view(R3, 3072, "p (b d) -> p b d", shape=(3, 512), b=3)
        hs = view(R3, 0, "p (b d) -> p b d", shape=(3, D), b=3)
        histRows = view(R3, 3072, shape=(512,))
        maskIn = view(R3, 3584, "p (l t) -> p l t", shape=(NLEV, 128), l=NLEV)
        h2f = view(R3, 0, "p (b d) -> p b d", shape=(2, D), b=2)
        kTok = view(R3, 1280, "p (n d) -> p n d", shape=(12, 128), n=12)
        stP = view(R3, 0, "p (h d) -> p h d", shape=(4, 128), h=4)
        tailT = view(R3, 2560, shape=(512,))
        x2T = view(R3, 3072, "p (k t) -> p k t", shape=(8, 128), k=8)
        ga, gs, gu, gt, xgs, xgT, hidT, ysb, hid = [view(R3, 512 * n, shape=(512,)) for n in range(9)]
        cv = view(R4, 0, "p (c t) -> p c t", shape=(4, NT), c=4)
        u = view(R4, 1280, "p (c t) -> p c t", shape=(4, NT + 2 + 2 * NSEQ), c=4)
        junk = view(R4, 0, shape=(D,))
        bias3 = R4[:, 0:1536].bitcast(bf16).rearrange("p (m d) -> p m d", m=3)
        G = view(R4, 1536, "p (b s) -> p b s", shape=(3, 128), b=3)
        oh = view(R4, 1536, "p (b k e) -> p b k e", shape=(3, TOPK, E), b=3, k=TOPK)
        GT = view(R4, 1920, "p (n t) -> p n t", shape=(2, NT), n=2)

        consts = sb("consts", [128, 128 * 4 + 34 + 8 + 8 + 32])
        ident, tri, ones, iota2 = [consts[:, 128 * n:128 * n + 128] for n in range(4)]
        expCol = consts[:, 512:546]
        roundStart = consts[:, 546:554]
        seqMask = consts[:, 554:562]
        expId = consts[:, 562:594]
        levMask = sb("levMask", [128, NLEV, 128], u8)
        trib = sb("trib", [128, 128], bf16)
        onesb = sb("onesb", [128, 128], bf16)
        rw = sb("rw", [128, 8, E])
        rb = sb("rb", [128, E])
        parRows = sb("parRows", [44, 128])
        par = sb("par", [128, 44])
        lbW = sb("lbW", [128, 5, 4])
        lb = sb("lb", [128, 4])
        oml = sb("oml", [128, 4])
        epsT = sb("epsT", [128, 1])
        tail = sb("tail", [128, 4, 18])
        st = sb("st", [128, 24])
        f8 = sb("f8", [128, 4, NSEQ])
        lg = sb("lg", [128, 3, E])
        mx = sb("mx", [128, 3, 8])
        mi = sb("mi", [128, 3, 8], u32)
        mif = sb("mif", [128, 3, 8])
        ex = sb("ex", [128, 3, 4])
        comb = sb("comb", [128, 3, E + 1])
        sel = sb("sel", [128, 3, E], bf16)
        posm = sb("posm", [128, 3, E + 1])
        cmax = sb("cmax", [128, 1])
        flag = sb("flag", [128, 8], i32)
        P = sb("P", [128, 3, SLOTS], bf16)
        eh = sb("eh", [128, 2, SLOTS], bf16)

        ps = ctx.enter_context(nc.psum_tensor("ps", [128, 8, 512], f32))

        def banks(a, n, rows, cols):
            return ps[0:rows, a:a + n, 0:cols]

        ringIn = [sem(f"ring_in{s}") for s in range(NR)]
        xIn = [sem(f"x_in{b}") for b in range(3)]
        constIn, maskInSem, parIn, routerIn, histIn = sem("const_in"), sem("mask_in"), sem("par_in"), sem("router_in"), sem("hist_in")
        s0In, biasIn, fnwIn = sem("s0_in"), sem("bias_in"), sem("fnw_in")
        s0Out, stOut, tailOut, yOut = sem("s0_out"), sem("state_out"), sem("tail_out"), sem("y_out")
        parMM, xTMM, projMM, levMM, oMM = sem("par_mm"), sem("xT_mm"), sem("proj_mm"), sem("lev_mm"), sem("o_mm")
        ssMM, kTokMM, stPMM, stSMM, tailMM = sem("ss_mm"), sem("ktok_mm"), sem("stp_mm"), sem("sts_mm"), sem("tail_mm")
        woutMM, x2TMM, lgMM, posMM = sem("wout_mm"), sem("x2T_mm"), sem("lg_mm"), sem("pos_mm")
        wUsed = sem("w_used")
        xgMM, gtMM, xgTMM, hidTMM, scatMM = sem("xg_mm"), sem("gt_mm"), sem("xgT_mm"), sem("hidT_mm"), sem("scat_mm")
        unitOut = [sem(f"unit_out{n}") for n in range(2)]
        ssqDone, rootDone, expDone = sem("ssq_done"), sem("root_done"), sem("lbexp_done")
        gSig, crossOut, oSq, oRoot = sem("gsig"), sem("cross_out"), sem("osq"), sem("oroot")
        kTokOut, tailTOut = sem("ktok_out"), sem("tailT_out")
        ssq2Done, root2Done, x2TOut, exDone, partDone = (sem("ssq2"), sem("root2"), sem("x2T_out"), sem("ex_done"),
                                                          sem("part_done"))
        sigDone, xgOut, gtOut, hidTOut, yEvac = sem("sig_done"), sem("xg_out"), sem("gt_out"), sem("hidT_out"), sem("y_evac")
        finSq, finRoot = sem("fin_sq"), sem("fin_root")
        step = sem("dve_step")
        parOut, hsDone, hTOut, levOut, kScaled = sem("par_out"), sem("hs_done"), sem("hT_out"), sem("lev_out"), sem("k_scaled")
        f8Out, mixDone, stPOut, stSOut = sem("f8_out"), sem("mix_done"), sem("stp_out"), sem("sts_out")
        x2Done, resid, lgOut, mxDone, selDone, posOut = (sem("x2_done"), sem("resid"), sem("lg_out"), sem("mx_done"),
                                                         sem("sel_done"), sem("pos_out"))
        h2Parts, flagDone, histOut, epsOut, maskOut = sem("h2_parts"), sem("flag_done"), sem("hist_out"), sem("eps_out"), sem("mask_out")
        prep, aDone, uDone, tDone, hidDone, xgTOut, accDone = (sem("prep"), sem("a_done"), sem("u_done"), sem("t_done"),
                                                               sem("hid_done"), sem("xgT_out"), sem("acc_done"))
        posShift, zeroed, moeDone, finDone = sem("pos_shift"), sem("zeroed"), sem("moe_done"), sem("fin_done")
        aloneP, aloneV, aloneT = sem("alone_pool"), sem("alone_dve"), sem("alone_pe")
        warm = sem("warm")
        vSelDone, s0Scaled, tailIn, biasDone, biasPart, biasRest, ehDone = (sem("vsel_done"), sem("s0_scaled"), sem("tail_in"),
                                                                  sem("bias_done"), sem("bias_part"), sem("bias_rest"), sem("eh_done"))

        w_in = A["w_in"][0].rearrange("(k p) n -> p k n", p=128)
        w_out = A["w_out"][0].rearrange("(k p) n -> p k n", p=128)
        w_exp = [A[n][0].rearrange("e (k p) n -> e p k n", p=128) for n in ("w_gate", "w_up", "w_down")]
        b_exp = [A[n][0] for n in ("b_gate", "b_up", "b_down")]
        s0 = ring[:, L_S0:L_S0 + 2, :].rearrange("p s (n d) -> p (s n) d", d=128)
        s0v = s0.rearrange("p (b h) d -> p b h d", h=NH)
        biasRaw = ring[:, L_BIAS % NR:L_BIAS % NR + 2, :].rearrange("p s n -> p (s n)")

        def slot_k(L, cols):
            return ring[:, L % NR, :].rearrange("p (k n) -> p k n", n=cols)

        START = 1

        def credit(eng, *sems):
            for s in sems:
                eng.sem_inc(s, START)

        block = ctx.enter_context(nc.Block())

        @block.sync
        def _(sp):
            def load_expert(e, j, s):
                m, c = divmod(j, 4)
                sp.dma_start(ring[:, s, :].rearrange("p (k n) -> p k n", n=D),
                             w_exp[m][e, :, 2 * c:2 * c + 2, :]).then_inc(ringIn[s], 16)

            def load_in(L, col):
                sp.dma_start(slot_k(L, 256), w_in[:, :, 256 * col:256 * col + 256]).then_inc(ringIn[L % NR], 16)

            for b, (t0, n) in enumerate(TOK):
                src = A["x_prompt"][0, t0:t0 + n, :] if b < 2 else A["x_sample"].rearrange("s t d -> (s t) d")
                sp.dma_start(x[0:n, b, :], src).then_inc(xIn[b], 16)
            sp.dma_start(consts[:], A["consts"]).then_inc(constIn, 16)
            for kind in ("f", "q", "i", "g"):
                for j in range(2):
                    load_in(W_CHUNK[kind][0] + j, W_CHUNK[kind][1] + j)
            sp.dma_start(s0, A["state_hgrn"][0].rearrange("b h k v -> k (b h) v")).then_inc(s0In, 16)
            for kind in ("cg", "vc", "bg"):
                for j in range(2):
                    load_in(W_CHUNK[kind][0] + j, W_CHUNK[kind][1] + j)
            sp.wait_ge(projMM, load_done(1))
            for m in range(3):
                for part in range(4):
                    sp.dma_start(biasRaw[32 * part:32 * part + 32, D * m:D * m + D], b_exp[m]).then_inc(biasIn, 16)
            for c in range(4):
                sp.wait_ge(projMM, load_done(L_WOUT + c - NR))
                sp.dma_start(slot_k(L_WOUT + c, D), w_out[:, 2 * c:2 * c + 2, :]).then_inc(ringIn[(L_WOUT + c) % NR], 16)
            for n in range(LPE * PER_BODY):
                L = L_EXP + n
                before = L - NR
                if before in (L_S0, L_S0 + 1):
                    sp.wait_ge(s0Out, 16)
                elif before in (L_BIAS, L_BIAS + 1):
                    sp.wait_ge(biasDone, 1)
                elif before < L_WOUT:
                    sp.wait_ge(projMM, load_done(before))
                elif before < L_EXP:
                    sp.wait_ge(woutMM, 3)
                else:
                    sp.wait_ge(wUsed, n - NR + 1 + START)
                load_expert(n // LPE, n % LPE, L % NR)

            def body(first, it):
                for n in range(LPE * PER_BODY):
                    sp.wait_ge(wUsed, (first + (n - NR + 1)) + it * (LPE * PER_BODY) + START)
                    load_expert(it * PER_BODY + n // LPE, n % LPE, (L_EXP + n) % NR)

            with sp.Fori(1, BODIES) as it:
                body(0, it)
            sp.wait_ge(flagDone, 1)
            with sp.Fori(1, ROUNDS) as r:
                more = sp.value_load(flag[0:1, bass.ds(r, 1)], min_val=0, max_val=1)
                with sp.If(more != 0):
                    with sp.Fori(0, BODIES) as it:
                        body(r * (LPE * E), it)
                    sp.nop()
                with sp.Else():
                    sp.nop()
            yp = A["y_prompt"][0].rearrange("(b p) d -> b p d", p=128)
            for b, (t0, n) in enumerate(TOK):
                sp.wait_ge(finDone, b + 1)
                dst = yp[b] if b < 2 else A["y_sample"].rearrange("s t d -> (s t) d")
                sp.dma_start(dst, yout[0:n, b, :]).then_inc(yOut, 16)
            sp.wait_ge(yOut, 48)
            sp.wait_ge(s0Out, 16)
            sp.wait_ge(stOut, 16)
            sp.wait_ge(tailOut, 32)

        @block.gpsimd
        def _(pool):
            credit(pool, ehDone)
            pool.dma_start(rw[:], A["router_w"][0].rearrange("(k p) e -> p k e", p=128)).then_inc(routerIn, 16)
            pool.dma_start(rb[:], A["router_b"][0].partition_broadcast(128)).then_inc(routerIn, 16)
            for h in range(NH):
                if h == 0:
                    pool.wait_ge(oMM, NH)
                    pool.wait_ge(f8Out, 1)
                if h == 1:
                    pool.wait_ge(kTokMM, 1)
                if h >= 2:
                    pool.wait_ge(stSMM, h - 1)
                pool.tensor_tensor(vSel[h % 2][0:64], v[0:64, 2, 128 * h:128 * h + 128].unsqueeze(1).broadcast_to([64, 8, 128]),
                                   seqMask[0:64, :].unsqueeze(2).broadcast_to([64, 8, 128]), ALU.mult).then_inc(vSelDone, 1)
                pool.tensor_tensor(s0v[:, :, h, :], s0v[:, :, h, :], f8[:, h, :].unsqueeze(2).broadcast_to([128, 8, 128]),
                                   ALU.mult).then_inc(s0Scaled, 1)
            pool.wait_ge(stSOut, NH)
            pool.dma_start(A["new_hgrn_sample"][0].rearrange("b h k v -> k (b h) v"), s0).then_inc(s0Out, 16)
            for n in range(2):
                pool.wait_ge(unitOut[n], len(UNITS) // 2)
            pool.tensor_copy(tail[:, :, 0:2], u[:, :, NP:NP + 2])
            pool.tensor_copy(tail[:, :, 2:18].rearrange("p c (s w) -> p c s w", w=2),
                             u[:, :, NP + 2:].rearrange("p c (s w) -> p c s w", w=10)[:, :, :, 8:10]).then_inc(tailIn, 1)
            pool.wait_ge(woutMM, 3)
            pool.dma_start(fnw, A["final_norm_w"].partition_broadcast(128)).then_inc(fnwIn, 16)

            def pick(value, par):
                pool.sem_inc(aloneP, 1)
                pool.tensor_copy(eh[:, par, :], expCol[:, value].broadcast_to([128, SLOTS])).then_inc(ehDone, 1)

            pool.wait_ge(flagDone, 1)
            pool.wait_ge(tailIn, 1)
            with pool.Fori(0, ROUNDS) as r:
                more = pool.value_load(flag[0:1, bass.ds(r, 1)], min_val=0, max_val=1)
                with pool.If(more != 0):
                    pool.wait_ge(ehDone, r * (E + 1) + START)
                    pool.wait_ge(wUsed, r * (LPE * E) + START)
                    pick(slice(0, 1), 0)
                    with pool.Fori(0, BODIES) as it:
                        for j in range(PER_BODY):
                            pool.wait_ge(wUsed, r * (LPE * E) + (it * (LPE * PER_BODY) + LPE * j) + START)
                            pick(bass.ds(it * PER_BODY + (j + 1), 1), (j + 1) % 2)
                    pool.nop()
                with pool.Else():
                    pool.nop()

        @block.scalar
        def _(act):
            credit(act, sigDone, xgOut, gtOut, hidTOut, yEvac)
            rows = [("lb_logits", 8), ("conv_w", 12), ("conv_b", 4), ("gnorm_w", 4), ("norm_mix_w", 8), ("norm_ffn_w", 8)]
            at = 0
            for name, n in rows:
                act.dma_start(parRows[at:at + n, :], A[name]).then_inc(parIn, 16)
                at += n
            act.dma_start(histRows[0:16, :], A["state_conv"][0].rearrange("b w c -> (b w) c")).then_inc(histIn, 16)
            act.dma_start(maskIn, A["lev_mask"]).then_inc(maskInSem, 16)
            for b, (t0, n) in enumerate(TOK):
                act.wait_ge(xIn[b], 16)
                if b:
                    act.wait_ge(ssqDone, b)
                act.activation(junk[0:n], x[0:n, b, :], ACT.Square, accum_out=st[0:n, b:b + 1]).then_inc(ssqDone, 1)
            act.wait_ge(epsOut, 1)
            for b, (t0, n) in enumerate(TOK):
                act.wait_ge(ssqDone, b + 1)
                act.activation(st[0:n, 3 + b:4 + b], st[0:n, b:b + 1], ACT.Sqrt, bias=epsT[0:n, :], scale=1.0 / D)\
                   .then_inc(rootDone, 1)
            act.wait_ge(parOut, 2)
            act.activation(lbW[:, 1:3, :], lbW[:, 1:3, :], ACT.Exp).then_inc(expDone, 1)
            for item in SCHED:
                kind = item[0]
                if kind in ("f", "q", "i", "g", "cg"):
                    n = UIDX[item]
                    src = ps[:, n % 2, 0:NT]
                    act.wait_ge(projMM, n + 1)
                    out = unitOut[n % 2]
                if kind == "f":
                    h = item[1]
                    act.activation(fdec[:, h, :], src, ACT.Sigmoid)
                    act.activation(kS[:, h, :], src, ACT.Sigmoid, scale=-1.0).then_inc(out, 1)
                elif kind == "q":
                    act.activation(q[:, item[1], :], src, ACT.Copy).then_inc(out, 1)
                elif kind == "i":
                    _, c, b = item
                    act.wait_ge(maskOut, 1)
                    act.activation(v[0:TOK[b][1], b, 256 * c:256 * c + 256], ps[0:TOK[b][1], n % 2, 0:256], ACT.Copy)\
                       .then_inc(out, 1)
                elif kind == "g":
                    act.activation(g[:, item[1], :], src, ACT.Sigmoid).then_inc(gSig, 1)
                elif kind == "cg":
                    act.activation(cv[:, item[1], :], src, ACT.Copy).then_inc(out, 1)
                elif kind == "cross":
                    act.wait_ge(levMM, 2 * (NLEV + 1) + 1)
                    act.activation(sc[:, :, 256:384], ps[:, 6, :].rearrange("p (h t) -> p h t", h=4), ACT.Copy)\
                       .then_inc(crossOut, 1)
                elif kind == "o":
                    h = item[1]
                    act.wait_ge(oMM, h + 1)
                    act.activation(sc[:, h, 0:NT], ps[:, 2 + h, 0:NT], ACT.Square).then_inc(oSq, 1)
                elif kind == "ss":
                    h = item[1]
                    act.wait_ge(ssMM, h + 1)
                    act.activation(sc[:, h, 0:NT], ps[:, 6 + h % 2, 0:NT], ACT.Sqrt, bias=epsT[:], scale=1.0 / 128).then_inc(oRoot, 1)
                elif kind == "ktok":
                    act.wait_ge(kTokMM, 1)
                    act.wait_ge(mixDone, NH)
                    act.activation(kTok[:, 0:8, :].rearrange("p n d -> p (n d)"), ps[:, 6:8, :].rearrange("p a n -> p (a n)"),
                                   ACT.Copy)
                    act.activation(kTok[0:64, 8:12, :].rearrange("p n d -> p (n d)"), ps[0:64, 2, :], ACT.Copy).then_inc(kTokOut, 1)
                elif kind == "stp":
                    act.wait_ge(stPMM, 1)
                    act.activation(stP.rearrange("p h d -> p (h d)"), ps[:, 3, :], ACT.Copy).then_inc(stPOut, 1)
            act.wait_ge(stPOut, 1)
            act.dma_start(A["new_hgrn_prompt"][0, 0].rearrange("h k v -> k h v"), stP).then_inc(stOut, 16)
            b3 = bias3.rearrange("p m d -> p (m d)")
            act.wait_ge(biasIn, 16 * 12)
            act.wait_ge(tailIn, 1)
            act.activation(b3, biasRaw[:, 0:3 * D], ACT.Copy).then_inc(biasPart, 1)
            act.wait_ge(biasRest, 1)
            act.activation(b3[64:128], biasRaw[64:128, 0:3 * D], ACT.Copy).then_inc(biasPart, 1)
            act.wait_ge(biasRest, 2)
            act.activation(b3[96:128], biasRaw[96:128, 0:3 * D], ACT.Copy).then_inc(biasDone, 1)
            act.wait_ge(tailMM, 1)
            act.activation(tailT[0:18, :], ps[0:18, 2, :], ACT.Copy).then_inc(tailTOut, 1)
            act.wait_ge(tailTOut, 1)
            act.dma_start(A["new_conv_prompt"][0, 0], tailT[0:2, :]).then_inc(tailOut, 16)
            act.dma_start(A["new_conv_sample"][0].rearrange("b w c -> (b w) c"), tailT[2:18, :]).then_inc(tailOut, 16)

            act.wait_ge(stOut, 16)
            for b, (t0, n) in enumerate(TOK):
                act.wait_ge(x2Done, b + 1)
                if b == 2:
                    act.wait_ge(h2Parts, 1)
                act.activation(h2f[0:n, b % 2, :], x[0:n, b, :], ACT.Square, accum_out=st[0:n, 9 + b:10 + b]).then_inc(ssq2Done, 1)
                act.wait_ge(ssq2Done, b + 1)
                act.activation(st[0:n, 12 + b:13 + b], st[0:n, 9 + b:10 + b], ACT.Sqrt, bias=epsT[0:n, :], scale=1.0 / D)\
                   .then_inc(root2Done, 1)
                if b == 2:
                    act.wait_ge(root2Done, 3)
                    act.activation(st[0:64, 18:19], st[0:64, 14:15], ACT.Exp).then_inc(warm, 1)
                act.wait_ge(resid, 2 * b + 1)
                act.activation(h2p[0:n, 0, b, :], h2f[0:n, b % 2, :], ACT.Copy).then_inc(partDone, 1)
                act.wait_ge(resid, 2 * b + 2)
                act.activation(h2p[0:n, 1, b, :], h2f[0:n, b % 2, :], ACT.Copy).then_inc(partDone, 1)
            act.wait_ge(mxDone, 3)
            act.activation(ex[:], lg[:, :, 0:4], ACT.Exp).then_inc(exDone, 1)
            act.wait_ge(warm, 1)
            act.activation(st[0:64, 18:19], st[0:64, 14:15], ACT.Sigmoid).then_inc(warm, 1)

            act.wait_ge(tailOut, 32)
            act.wait_ge(flagDone, 1)
            with act.Fori(0, ROUNDS) as r:
                more = act.value_load(flag[0:1, bass.ds(r, 1)], min_val=0, max_val=1)
                with act.If(more != 0):
                    p0, e0 = r * (E + 1), r * E

                    def prefetch(m, scattered, par):
                        act.wait_ge(xgMM, m + 1 + START)
                        act.wait_ge(xgTMM, m + START)
                        act.activation(xgs, ps[:, 3, :], ACT.Copy).then_inc(xgOut, 1)
                        act.wait_ge(gtMM, m + 1 + START)
                        act.wait_ge(scatMM, scattered + START)
                        act.activation(GT[:, par, :], ps[:, 5, 0:NT], ACT.Copy).then_inc(gtOut, 1)

                    prefetch(p0, p0 * 3, 0)
                    with act.Fori(0, BODIES) as it:
                        for j in range(PER_BODY):
                            e = e0 + (it * PER_BODY + j)
                            m = p0 + (it * PER_BODY + (j + 1))
                            act.wait_ge(aDone, e + 1 + START)
                            act.wait_ge(hidDone, e + START)
                            act.activation(gs, ga, ACT.Sigmoid, scale=ALPHA).then_inc(sigDone, 1)
                            prefetch(m, m * 3, (j + 1) % 2)
                            act.wait_ge(hidTMM, e + 1 + START)
                            act.wait_ge(wUsed, e * LPE + START)
                            act.activation(hidT, ps[:, 4, :], ACT.Copy).then_inc(hidTOut, 1)
                            act.wait_ge(wUsed, e * LPE + LPE + START)
                            act.wait_ge(scatMM, m * 3 + START)
                            act.activation(ysb, ps[:, 2, :], ACT.Copy).then_inc(yEvac, 1)
                    act.nop()
                with act.Else():
                    act.nop()
            act.wait_ge(moeDone, 1)
            for b, (t0, n) in enumerate(TOK):
                if b:
                    act.wait_ge(finSq, b)
                act.activation(junk2[0:n], x[0:n, b, :], ACT.Square, accum_out=st[0:n, b:b + 1]).then_inc(finSq, 1)
                act.wait_ge(finSq, b + 1)
                act.activation(st[0:n, 3 + b:4 + b], st[0:n, b:b + 1], ACT.Sqrt, bias=epsT[0:n, :], scale=1.0 / D)\
                   .then_inc(finRoot, 1)

        @block.vector
        def _(dve):
            count = {}

            def did(ins, s=step):
                ins.then_inc(s, 1)
                count[s.name] = count.get(s.name, 0) + 1
                return s, count[s.name]

            def need(*done):
                for s, n in done:
                    dve.wait_ge(s, n)

            credit(dve, zeroed, prep, aDone, uDone, tDone, hidDone, xgTOut, accDone)
            TT, TS, STT = dve.tensor_tensor, dve.tensor_scalar, dve.scalar_tensor_tensor
            did(dve.memset(epsT[:], EPS), epsOut)
            did(dve.memset(u[:, :, 0:2], 0.0))
            did(dve.memset(comb[:], 0.0))
            did(dve.memset(posm[:], 0.0))
            did(dve.memset(lg[:], 0.0))
            did(dve.memset(mif[:], 0.0))
            dve.wait_ge(constIn, 16)
            did(dve.tensor_copy(trib[:], tri))
            did(dve.tensor_copy(onesb[:], ones))
            for b, (t0, n) in enumerate(TOK):
                dve.wait_ge(rootDone, b + 1)
                need(did(dve.reciprocal(st[0:n, 6 + b:7 + b], st[0:n, 3 + b:4 + b])))
                TS(hs[0:n, b, :], x[0:n, b, :], st[0:n, 6 + b:7 + b], None, ALU.mult).then_inc(hsDone, 1)
            dve.wait_ge(parMM, 1)
            need(did(dve.tensor_copy(par[:], ps[:, 0, 0:44]), parOut))
            LB, CW, CB, GN, NM, NF = 0, 8, 20, 24, 28, 36
            did(dve.tensor_copy(u[:, :, NP + 2:].rearrange("p c (s w) -> p c s w", w=10)[:, :, :, 0:2],
                                ps[:, 1, 0:64].rearrange("p (c s w) -> p c s w", c=4, w=2)), histOut)
            need(did(TT(lbW[:, 0, :], par[:, LB:LB + 4], par[:, LB + 4:LB + 8], ALU.max)))
            did(TT(lbW[:, 1:3, :], par[:, LB:LB + 8].rearrange("p (a h) -> p a h", a=2),
                   lbW[:, 0, :].unsqueeze(1).broadcast_to([128, 2, 4]), ALU.subtract), parOut)
            for b, (t0, n) in enumerate(TOK):
                dve.wait_ge(xTMM, b + 1)
                TT(hT[:, :, t0:t0 + n], ps[:, 2 + 2 * b:4 + 2 * b, :].rearrange("p a (k t) -> p (a k) t", t=128)[:, :, 0:n],
                   par[:, NM:NM + 8].unsqueeze(2).broadcast_to([128, 8, n]), ALU.mult).then_inc(hTOut, 1)
            dve.wait_ge(expDone, 1)
            need(did(TT(lbW[:, 3, :], lbW[:, 1, :], lbW[:, 2, :], ALU.add)))
            need(did(dve.reciprocal(lbW[:, 4, :], lbW[:, 3, :])))
            need(did(TT(lb[:], lbW[:, 1, :], lbW[:, 4, :], ALU.mult)))
            need(did(TS(oml[:], lb[:], -1.0, 1.0, ALU.mult, ALU.add)))
            dve.wait_ge(maskInSem, 16)
            did(dve.tensor_copy(levMask[:], maskIn), maskOut)
            dve.wait_ge(routerIn, 32)
            did(TT(rw[:], rw[:], par[:, NF:NF + 8].unsqueeze(2).broadcast_to([128, 8, E]), ALU.mult))

            pairs = lambda ap, p: ap[:, 2 * p:2 * p + 2, :]
            fk, gk = {}, {}
            fp = {}
            convDone = {}
            for item in SCHED:
                kind = item[0]
                if kind in ("f", "g", "vc", "bg"):
                    n = UIDX[item]
                    src = ps[:, n % 2, :]
                if kind == "f":
                    h = item[1]
                    dve.wait_ge(unitOut[n % 2], n // 2 + 1)
                    did(TS(fdec[:, h, :], fdec[:, h, :], oml[:, h:h + 1], lb[:, h:h + 1], ALU.mult, ALU.add))
                    fk[h] = did(TS(kS[:, h, :], kS[:, h, :], oml[:, h:h + 1], None, ALU.mult), kScaled)
                elif kind == "g":
                    h = item[1]
                    dve.wait_ge(gSig, h + 1)
                    gk[h] = did(STT(g[:, h, :], src[:, 0:NT], par[:, GN + h:GN + h + 1], g[:, h, :], ALU.mult, ALU.mult), unitOut[n % 2])
                elif kind == "vc":
                    c = item[1]
                    m = UIDX[("cg", c)]
                    dve.wait_ge(unitOut[m % 2], m // 2 + 1)
                    dve.wait_ge(projMM, n + 1)
                    us = u[:, c, NP + 2:].rearrange("p (s w) -> p s w", w=10)
                    did(TT(u[:, c, 2:NP + 2], src[:, 0:NP], cv[:, c, 0:NP], ALU.mult))
                    TT(us[:, :, 2:10], src[:, NP:NT].rearrange("p (s w) -> p s w", w=8),
                       cv[:, c, NP:NT].rearrange("p (s w) -> p s w", w=8), ALU.mult).then_inc(unitOut[n % 2], 1)
                    dve.wait_ge(unitOut[n % 2], n // 2 + 1)
                    cp, cs = cv[:, c, 0:NP], cv[:, c, NP:NT].rearrange("p (s w) -> p s w", w=8)
                    w = lambda j: par[:, CW + 4 * j + c:CW + 4 * j + c + 1]
                    did(TS(cp, u[:, c, 0:NP], w(0), par[:, CB + c:CB + c + 1], ALU.mult, ALU.add))
                    done = did(TS(cs, us[:, :, 0:8], w(0), par[:, CB + c:CB + c + 1], ALU.mult, ALU.add))
                    for j in (1, 2):
                        need(done)
                        did(STT(cp, u[:, c, j:NP + j], w(j), cp, ALU.mult, ALU.add))
                        done = did(STT(cs, us[:, :, j:8 + j], w(j), cs, ALU.mult, ALU.add))
                    convDone[c] = done
                elif kind == "bg":
                    c = item[1]
                    dve.wait_ge(projMM, n + 1)
                    need(convDone[c])
                    TT(mixT[:, c, :], src[:, 0:NT], cv[:, c, :], ALU.mult).then_inc(unitOut[n % 2], 1)
                elif kind == "lev":
                    _, l, p = item
                    dve.wait_ge(levMM, 2 * l + p + 1)
                    pb = ps[:, 2 + 2 * p:4 + 2 * p, :]
                    tiles = pb[:, :, 0:256].rearrange("p h (b t) -> p h b t", b=2)
                    smp = pb[0:64, :, 256:320]
                    outT = pairs(sc, p)[:, :, 0:256].rearrange("p h (b t) -> p h b t", b=2)
                    outS = pairs(sc, p)[0:64, :, 384:448]
                    if l == 0:
                        did(TT(outT, tiles, ident.unsqueeze(1).unsqueeze(1).broadcast_to([128, 2, 2, 128]), ALU.mult))
                        need(did(TT(outS, smp, ident[0:64, 0:64].unsqueeze(1).broadcast_to([64, 2, 64]), ALU.mult)))
                        mq = [UIDX[("q", 2 * p)], UIDX[("q", 2 * p + 1)]]
                        need(fk[2 * p + 1])
                        for m in mq:
                            dve.wait_ge(unitOut[m % 2], m // 2 + 1)
                        fp[p] = did(TT(pairs(qP, p), pairs(q, p), pairs(fdec, p), ALU.mult), levOut)
                    else:
                        size = 1 << (l - 1)
                        for hh in range(2):
                            m_ = levMask[:, l - 1, :].unsqueeze(1).broadcast_to([128, 2, 128])
                            last = did(dve.copy_predicated(outT[:, hh], m_, tiles[:, hh]))
                        if l <= 3:
                            m_ = levMask[0:64, l - 1, 0:64].unsqueeze(1).broadcast_to([64, 2, 64])
                            last = did(dve.copy_predicated(outS, m_, smp))
                        need(last, fp[p])
                        cols = NT if size <= 4 else NP
                        blk = lambda ap: pairs(ap, p)[:, :, 0:cols].rearrange("p h (b two t) -> p h b two t", two=2, t=size)
                        nb = cols // (2 * size)
                        fv, qv, kv = blk(fdec), blk(qP), blk(kS)
                        shape = [128, 2, nb, size]
                        did(TT(qv[:, :, :, 1, :], qv[:, :, :, 1, :], fv[:, :, :, 0, size - 1:size].broadcast_to(shape), ALU.mult))
                        need(did(TT(kv[:, :, :, 0, :], kv[:, :, :, 0, :], fv[:, :, :, 1, size - 1:size].broadcast_to(shape), ALU.mult)))
                        fp[p] = did(TT(fv[:, :, :, 1, size - 1], fv[:, :, :, 1, size - 1], fv[:, :, :, 0, size - 1], ALU.mult), levOut)
                        if l == 3 and p == 1:
                            need(fp[0], fp[1])
                            did(dve.tensor_copy(f8[:], fdec[:, :, NP + 7:NT:8]), f8Out)
                elif kind == "ss":
                    h = item[1]
                    dve.wait_ge(oRoot, h + 1)
                    need(gk[h], did(dve.reciprocal(sc[:, h, 0:NT], sc[:, h, 0:NT])))
                    need(did(TT(g[:, h, :], g[:, h, :], sc[:, h, 0:NT], ALU.mult)))
                    TT(mixT[:, NH + h, :], ps[:, 2 + h, 0:NT], g[:, h, :], ALU.mult).then_inc(mixDone, 1)
                elif kind == "sts":
                    h = item[1]
                    dve.wait_ge(stSMM, h + 1)
                    dve.wait_ge(s0Scaled, h + 1)
                    TT(s0v[:, :, h, :], s0v[:, :, h, :], ps[:, 4:6, :].rearrange("p a (b d) -> p (a b) d", d=128), ALU.add)\
                        .then_inc(stSOut, 1)
                elif kind == "cross":
                    dve.wait_ge(levMM, 2 * (NLEV + 1) + 1)
                    need(fp[0], fp[1])
                    did(TT(kS[:, :, 0:128], kS[:, :, 0:128], fdec[:, :, 255:256].broadcast_to([128, 4, 128]), ALU.mult), levOut)
            dve.wait_ge(biasPart, 1)
            b3 = bias3.rearrange("p m d -> p (m d)")
            TT(biasRaw[64:128, 0:3 * D], biasRaw[64:128, 0:3 * D], b3[64:128], ALU.subtract).then_inc(biasRest, 1)
            dve.wait_ge(biasPart, 2)
            dve.wait_ge(biasRest, 1)
            TT(biasRaw[96:128, 0:3 * D], biasRaw[96:128, 0:3 * D], b3[96:128], ALU.subtract).then_inc(biasRest, 1)

            WB = [0, 2, 4]
            for b, (t0, n) in enumerate(TOK):
                dve.wait_ge(woutMM, b + 1)
                if b < 2:
                    TT(x[0:n, b, :], x[0:n, b, :], ps[0:n, WB[b]:WB[b] + 2, :].rearrange("p a n -> p (a n)"), ALU.add)\
                        .then_inc(x2Done, 1)
                else:
                    did(TT(x[0:n, b, 0:512], x[0:n, b, 0:512], ps[0:n, WB[b], :], ALU.add))
                    TT(x[0:n, b, 512:1024], x[0:n, b, 512:1024], ps[64:64 + n, WB[b], :], ALU.add).then_inc(x2Done, 1)
                rstd = st[0:n, 15 + b:16 + b]
                dve.wait_ge(x2TMM, b + 1)
                if b:
                    dve.wait_ge(lgMM, b)
                dve.tensor_copy(x2T[:, :, 0:n], ps[:, 6:8, :].rearrange("p a (k t) -> p (a k) t", t=128)[:, :, 0:n])\
                    .then_inc(x2TOut, 1)
                dve.wait_ge(root2Done, b + 1)
                need(did(dve.reciprocal(rstd, st[0:n, 12 + b:13 + b])))
                hf = h2f[0:n, b % 2, :]
                dve.wait_ge(x2Done, b + 1)
                TS(hf, x[0:n, b, :], rstd, None, ALU.mult).then_inc(resid, 1)
                dve.wait_ge(lgMM, b + 1)
                need(did(STT(lg[0:n, b, :], ps[0:n, 5, E * b:E * b + E], rstd, rb[0:n, :], ALU.mult, ALU.add)))
                need(did(dve.max(mx[0:n, b, :], lg[0:n, b, :])))
                need(did(dve.max_index(mi[0:n, b, :], mx[0:n, b, :], lg[0:n, b, :])))
                did(TS(lg[0:n, b, 0:4], mx[0:n, b, 0:4], mx[0:n, b, 0:1], None, ALU.subtract), mxDone)
                last = did(dve.tensor_copy(mif[0:n, b, :], mi[0:n, b, :]))
                dve.wait_ge(partDone, 2 * b + 1)
                TT(hf, hf, h2p[0:n, 0, b, :], ALU.subtract).then_inc(resid, 1)
                if b < 2:
                    dve.wait_ge(partDone, 2 * b + 2)
                    dve.wait_ge(resid, 2 * b + 2)
                    did(TT(h2p[0:n, 2, b, :], hf, h2p[0:n, 1, b, :], ALU.subtract), h2Parts)
            four = [128, 3, TOPK, E]
            need(last)
            need(did(TT(oh, expId.unsqueeze(1).unsqueeze(1).broadcast_to(four), mif[:, :, 0:4].unsqueeze(3).broadcast_to(four),
                        ALU.is_equal)))
            dve.wait_ge(exDone, 1)
            dve.wait_ge(warm, 2)
            need(did(dve.tensor_reduce(st[:, 18:21], ex[:], AX.X, ALU.add)))
            need(did(dve.reciprocal(st[:, 21:24], st[:, 18:21])))
            need(did(TT(ex[:], ex[:], st[:, 21:24].unsqueeze(2).broadcast_to([128, 3, 4]), ALU.mult)))
            need(did(TT(oh, oh, ex[:].unsqueeze(3).broadcast_to(four), ALU.mult)))
            need(did(dve.tensor_reduce(comb[:, :, 0:E], oh.rearrange("p b k e -> p b e k"), AX.X, ALU.add)))
            TS(sel[:], comb[:, :, 0:E], 0.0, None, ALU.is_gt).then_inc(selDone, 1)
            dve.wait_ge(partDone, 6)
            dve.wait_ge(resid, 6)
            did(TT(h2p[0:64, 2, 2, :], h2f[0:64, 0, :], h2p[0:64, 1, 2, :], ALU.subtract), h2Parts)
            dve.wait_ge(selDone, 1)
            dve.wait_ge(posMM, 1)
            for b, (t0, n) in enumerate(TOK):
                need(did(STT(posm[0:n, b, 0:E], ps[0:n, 5, 128 + E * b:128 + E * b + E], 1.0, sel[0:n, b, :], ALU.add, ALU.mult)))
            did(TS(posm[:], posm[:], float(SLOTS), None, ALU.add), posOut)
            need(did(dve.tensor_reduce(cmax[0:1, :], ps[0:1, 5, 256:256 + E], AX.X, ALU.max)))
            need(did(TS(flag[0:1, :], roundStart[0:1, :], cmax[0:1, 0:1], None, ALU.is_lt)))
            did(dve.memset(flag[0:1, 0:1], 1), flagDone)
            dve.wait_ge(flagDone, 1)
            dve.wait_ge(posOut, 1)
            dve.wait_ge(stOut, 16)
            dve.wait_ge(tailOut, 32)

            with dve.Fori(0, ROUNDS) as r:
                more = dve.value_load(flag[0:1, bass.ds(r, 1)], min_val=0, max_val=1)
                with dve.If(more != 0):
                    p0, e0 = r * (E + 1), r * E

                    def prepare(m, col):
                        dve.wait_ge(xgMM, m + START)
                        dve.wait_ge(gtMM, m + START)
                        for b, (t0, n) in enumerate(TOK):
                            TS(P[0:n, b, :], iota2[0:n, 0:SLOTS], posm[0:n, b, col], None, ALU.is_equal)
                            ins = TS(G[0:n, b, :], iota2[0:n, :], posm[0:n, b, col], comb[0:n, b, col], ALU.is_equal, ALU.mult)
                        ins.then_inc(prep, 1)

                    def gathered(m):
                        dve.wait_ge(xgTMM, m + 1 + START)
                        TT(xgT.rearrange("p (c a s) -> p c a s", c=4, a=2),
                           ps[:, 3, :].rearrange("p (c a s) -> p c a s", c=4, a=2),
                           par[:, NF:NF + 8].rearrange("p (a c) -> p c a", a=2).unsqueeze(3).broadcast_to([128, 4, 2, SLOTS]),
                           ALU.mult).then_inc(xgTOut, 1)

                    def add_rows(turn_no):
                        for b, (t0, n) in enumerate(TOK):
                            dve.wait_ge(scatMM, turn_no * 3 + (b + 1) + START)
                            dve.wait_ge(accDone, turn_no * 3 + b + START)
                            TT(x[0:n, b, :], x[0:n, b, :], ps[0:n, 6:8, :].rearrange("p a n -> p (a n)"), ALU.add)\
                                .then_inc(accDone, 1)

                    dve.wait_ge(accDone, p0 * 3 + START)
                    dve.sem_inc(aloneV, 1)
                    dve.memset(GT[:, 1, :], 0.0)
                    dve.memset(ysb, 0.0).then_inc(zeroed, 1)
                    TS(posm[:], posm[:], -float(SLOTS), None, ALU.add).then_inc(posShift, 1)
                    dve.wait_ge(posShift, r + 1)
                    prepare(p0, slice(0, 1))
                    gathered(p0)
                    with dve.Fori(0, BODIES) as it:
                        for j in range(PER_BODY):
                            e = e0 + (it * PER_BODY + j)
                            m = p0 + (it * PER_BODY + (j + 1))
                            prepare(m, bass.ds(it * PER_BODY + (j + 1), 1))
                            add_rows(p0 + (it * PER_BODY + j))
                            dve.wait_ge(wUsed, e * LPE + 4 + START)
                            TS(ga, ps[:, 0, :], LIMIT, None, ALU.min).then_inc(aDone, 1)
                            dve.wait_ge(wUsed, e * LPE + 8 + START)
                            TS(gu, ps[:, 1, :], LIMIT, -LIMIT, ALU.min, ALU.max).then_inc(uDone, 1)
                            dve.wait_ge(aDone, e + 1 + START)
                            dve.wait_ge(uDone, e + 1 + START)
                            STT(gt, gu, 1.0, ga, ALU.add, ALU.mult).then_inc(tDone, 1)
                            dve.wait_ge(sigDone, e + 1 + START)
                            dve.wait_ge(tDone, e + 1 + START)
                            dve.wait_ge(hidTMM, e + START)
                            TT(hid, gt, gs, ALU.mult).then_inc(hidDone, 1)
                            gathered(m)
                    add_rows(p0 + E)
                    dve.wait_ge(accDone, (p0 + E + 1) * 3 + START)
                    dve.wait_ge(xgTOut, (r + 1) * (E + 1) + START)
                    dve.sem_inc(aloneV, 1)
                with dve.Else():
                    dve.nop()
            dve.nop().then_inc(moeDone, 1)
            dve.wait_ge(fnwIn, 16)
            for b, (t0, n) in enumerate(TOK):
                dve.wait_ge(finRoot, b + 1)
                need(did(dve.reciprocal(st[0:n, 6 + b:7 + b], st[0:n, 3 + b:4 + b])))
                STT(yout[0:n, b, :], x[0:n, b, :], st[0:n, 6 + b:7 + b], fnw[0:n], ALU.mult, ALU.mult).then_inc(finDone, 1)

        @block.tensor
        def _(pe):
            MM, TR = pe.matmul, pe.transpose
            credit(pe, wUsed, xgMM, gtMM, xgTMM, hidTMM, scatMM)
            pe.wait_ge(parIn, 16 * 6)
            pe.wait_ge(histIn, 16)
            pe.wait_ge(constIn, 16)
            for c in range(4):
                TR(ps[:, 1, 16 * c:16 * c + 16], histRows[0:16, 128 * c:128 * c + 128], ident[0:16, 0:16])
            TR(ps[:, 0, 0:44], parRows[:], ident[0:44, 0:44]).then_inc(parMM, 1)
            for b, (t0, n) in enumerate(TOK):
                pe.wait_ge(hsDone, b + 1)
                for k in range(KT):
                    ins = TR(ps[:, 2 + 2 * b + k // 4, 128 * (k % 4):128 * (k % 4) + n], hs[0:n, b, 128 * k:128 * k + 128],
                             ident[0:n, 0:n])
                ins.then_inc(xTMM, 1)
            pe.wait_ge(hTOut, 3)
            pe.wait_ge(histOut, 1)
            for item in SCHED:
                kind = item[0]
                if item in UIDX:
                    n = UIDX[item]
                    l0 = W_CHUNK[kind][0]
                    if n >= 2:
                        pe.wait_ge(unitOut[n % 2], n // 2)
                    if kind == "i":
                        _, c, b = item
                        t0, nt = TOK[b]
                        L = l0 + c
                        pe.wait_ge(ringIn[L % NR], ring_value(L))
                        for k in range(KT):
                            ins = MM(ps[0:nt, n % 2, 0:256], hT[:, k, t0:t0 + nt], slot_k(L, 256)[:, k, :],
                                     start=(k == 0), stop=(k == KT - 1))
                    else:
                        L, half = l0 + item[1] // 2, item[1] % 2
                        pe.wait_ge(ringIn[L % NR], ring_value(L))
                        for k in range(KT):
                            ins = MM(ps[:, n % 2, 0:NT], slot_k(L, 256)[:, k, 128 * half:128 * half + 128], hT[:, k, :],
                                     start=(k == 0), stop=(k == KT - 1))
                    ins.then_inc(projMM, 1)
                elif kind == "lev":
                    _, l, p = item
                    if l == 0:
                        for kk in ("f", "q"):
                            for h in (2 * p, 2 * p + 1):
                                m = UIDX[(kk, h)]
                                pe.wait_ge(unitOut[m % 2], m // 2 + 1)
                        pe.wait_ge(kScaled, 2 * p + 2)
                    else:
                        pe.wait_ge(levOut, 2 * (l - 1) + p + 1)
                    src = q if l == 0 else qP
                    for hh in range(2):
                        h = 2 * p + hh
                        for b in range(2):
                            ins = MM(ps[:, 2 + h, 128 * b:128 * b + 128], kS[:, h, 128 * b:128 * b + 128],
                                     src[:, h, 128 * b:128 * b + 128], start=True, stop=True)
                        if l <= 3:
                            ins = MM(ps[0:64, 2 + h, NP:NT], kS[:, h, NP:NT], src[:, h, NP:NT], start=True, stop=True)
                    ins.then_inc(levMM, 1)
                elif kind == "cross":
                    pe.wait_ge(levOut, 2 * (NLEV + 1))
                    for h in range(NH):
                        ins = MM(ps[:, 6, 128 * h:128 * h + 128], kS[:, h, 0:128], qP[:, h, 128:256], start=True, stop=True)
                    ins.then_inc(levMM, 1)
                elif kind == "o":
                    h = item[1]
                    if h == 0:
                        pe.wait_ge(crossOut, 1)
                        pe.wait_ge(s0In, 16)
                    o = ps[:, 2 + h, :]
                    hv = slice(128 * h, 128 * h + 128)
                    MM(o[:, 0:128], v[:, 0, hv], sc[:, h, 0:128], start=True, stop=False, skip_group_check=True)
                    MM(o[:, 128:256], v[:, 0, hv], sc[:, h, 256:384], start=False, stop=False, skip_group_check=True)
                    MM(o[:, 128:256], v[:, 1, hv], sc[:, h, 128:256], start=False, stop=False, skip_group_check=True)
                    MM(o[:, NP:NT], v[0:64, 2, hv], sc[0:64, h, 384:448], start=False, stop=False, skip_group_check=True)
                    for s in range(NSEQ):
                        t = NP + LS * s
                        ins = MM(o[:, t:t + LS], s0v[:, s, h, :], qP[:, h, t:t + LS], start=False, stop=True, skip_group_check=True)
                    ins.then_inc(oMM, 1)
                elif kind == "ss":
                    h = item[1]
                    pe.wait_ge(oSq, h + 1)
                    if h >= 2:
                        pe.wait_ge(oRoot, h - 1)
                    MM(ps[:, 6 + h % 2, 0:NT], ones, sc[:, h, 0:NT], start=True, stop=True).then_inc(ssMM, 1)
                elif kind == "ktok":
                    pe.wait_ge(oRoot, NH)
                    pe.wait_ge(levOut, 2 * (NLEV + 1) + 1)
                    pe.wait_ge(mixDone, 1)
                    for h in range(NH):
                        for b in range(2):
                            TR(ps[:, 6 + h // 2, 256 * (h % 2) + 128 * b:256 * (h % 2) + 128 * b + 128],
                               kS[:, h, 128 * b:128 * b + 128], ident)
                    for h in range(NH):
                        ins = TR(ps[0:64, 2, 128 * h:128 * h + 128], kS[:, h, NP:NT], ident)
                    ins.then_inc(kTokMM, 1)
                elif kind == "stp":
                    pe.wait_ge(kTokOut, 1)
                    pe.wait_ge(mixDone, NH)
                    for h in range(NH):
                        for b in range(2):
                            ins = MM(ps[:, 3, 128 * h:128 * h + 128], kTok[:, 2 * h + b, :], v[:, b, 128 * h:128 * h + 128],
                                     start=(b == 0), stop=(b == 1))
                    ins.then_inc(stPMM, 1)
                elif kind == "sts":
                    h = item[1]
                    pe.wait_ge(vSelDone, h + 1)
                    if h:
                        pe.wait_ge(stSOut, h)
                    for a in range(2):
                        ins = MM(ps[:, 4 + a, :], kTok[0:64, 8 + h, :],
                                 vSel[h % 2][0:64, 4 * a:4 * a + 4, :].rearrange("p b d -> p (b d)"), start=True, stop=True)
                    ins.then_inc(stSMM, 1)

            def tails():
                pe.wait_ge(tailIn, 1)
                for c in range(4):
                    ins = TR(ps[0:18, 2, 128 * c:128 * c + 128], tail[:, c, :], ident)
                ins.then_inc(tailMM, 1)

            def wout(b):
                t0, n = TOK[b]
                for k in range(KT):
                    L = L_WOUT + k // 2
                    w = slot_k(L, D)[:, k % 2, :]
                    if b == 0 and k % 2 == 0:
                        pe.wait_ge(ringIn[L % NR], ring_value(L))
                    for half in range(2):
                        dst = ps[0:n, 2 * b + half, :] if b < 2 else ps[64 * half:64 * half + 64, 4, :]
                        ins = MM(dst, mixT[:, k, t0:t0 + n], w[:, 512 * half:512 * half + 512], start=(k == 0), stop=(k == KT - 1))
                ins.then_inc(woutMM, 1)

            def logits(b):
                t0, n = TOK[b]
                pe.wait_ge(x2Done, b + 1)
                if b:
                    pe.wait_ge(x2TOut, b)
                for k in range(KT):
                    ins = TR(ps[:, 6 + k // 4, 128 * (k % 4):128 * (k % 4) + n], x[0:n, b, 128 * k:128 * k + 128], ident[0:n, 0:n])
                ins.then_inc(x2TMM, 1)
                pe.wait_ge(x2TOut, b + 1)
                for k in range(KT):
                    ins = MM(ps[0:n, 5, E * b:E * b + E], x2T[:, k, 0:n], rw[:, k, :], start=(k == 0), stop=(k == KT - 1))
                ins.then_inc(lgMM, 1)

            pe.wait_ge(mixDone, NH)
            pe.wait_ge(unitOut[0], len(UNITS) // 2)
            pe.wait_ge(unitOut[1], len(UNITS) // 2)
            wout(0)
            tails()
            pe.wait_ge(tailTOut, 1)
            pe.wait_ge(stPOut, 1)
            wout(1)
            logits(0)
            pe.wait_ge(stSOut, NH)
            wout(2)
            logits(1)
            logits(2)
            pe.wait_ge(selDone, 1)
            for b, (t0, n) in enumerate(TOK):
                for a in range(b):
                    MM(ps[0:n, 5, 128 + E * b:128 + E * b + E], onesb[:, 0:n], sel[:, a, :], start=(a == 0), stop=False)
                MM(ps[0:n, 5, 128 + E * b:128 + E * b + E], trib[0:n, 0:n], sel[0:n, b, :], start=(b == 0), stop=True)
            for b, (t0, n) in enumerate(TOK):
                ins = MM(ps[:, 5, 256:256 + E], onesb[0:n, :], sel[0:n, b, :], start=(b == 0), stop=(b == 2))
            ins.then_inc(posMM, 1)
            pe.wait_ge(h2Parts, 3)
            pe.wait_ge(biasDone, 1)
            pe.wait_ge(flagDone, 1)

            with pe.Fori(0, ROUNDS) as r:
                more = pe.value_load(flag[0:1, bass.ds(r, 1)], min_val=0, max_val=1)
                with pe.If(more != 0):
                    p0, e0 = r * (E + 1), r * E

                    def gather(m):
                        pe.wait_ge(prep, m + 1 + START)
                        pe.wait_ge(xgTOut, m + START)
                        for b, (t0, n) in enumerate(TOK):
                            for part in range(3):
                                for half in range(2):
                                    ins = MM(ps[64 * half:64 * half + 64, 3, :], P[0:n, b, :],
                                             h2p[0:n, part, b, 512 * half:512 * half + 512],
                                             start=(b == 0 and part == 0), stop=(b == 2 and part == 2))
                        ins.then_inc(xgMM, 1)

                    def turn_gates(m):
                        pe.wait_ge(gtOut, m + START)
                        for b, (t0, n) in enumerate(TOK):
                            ins = TR(ps[:, 5, t0:t0 + n], G[0:n, b, :], ident[0:n, 0:n])
                        ins.then_inc(gtMM, 1)

                    def turn(m):
                        pe.wait_ge(xgOut, m + 1 + START)
                        for c in range(4):
                            ins = TR(ps[:, 3, 128 * c:128 * c + 128], xgs[:, 128 * c:128 * c + 128], ident)
                        ins.then_inc(xgTMM, 1)

                    def scatter(b, turn_no, par):
                        t0, n = TOK[b]
                        pe.wait_ge(accDone, turn_no * 3 + b + START)
                        if n == 64:
                            pe.sem_inc(aloneT, 1)
                        for half in range(2):
                            ins = MM(ps[0:n, 6 + half, :], GT[64 * half:64 * half + 64, par, t0:t0 + n],
                                     ysb[64 * half:64 * half + 64, :], start=True, stop=True)
                        ins.then_inc(scatMM, 1)

                    def product(mat, bank, lhs, e, it, j, between=()):
                        for half in range(2):
                            MM(ps[64 * half:64 * half + 64, bank, :], eh[:, j % 2, :], bias3[:, mat, 512 * half:512 * half + 512],
                               start=True, stop=False)
                        for k in range(KT):
                            n = LPE * j + 4 * mat + k // 2
                            s = (L_EXP + n) % NR
                            if k % 2 == 0:
                                pe.wait_ge(ringIn[s], (r * BODIES + it) * (16 * PER_BODY * LPE // NR) + ring_value(L_EXP + n))
                            w = ring[:, s, D * (k % 2):D * (k % 2) + D]
                            for half in range(2):
                                ins = MM(ps[64 * half:64 * half + 64, bank, :], lhs(k), w[:, 512 * half:512 * half + 512],
                                         start=False, stop=(k == KT - 1))
                            if k % 2:
                                ins.then_inc(wUsed, 1)
                                if k // 2 < len(between):
                                    between[k // 2]()

                    half_c = lambda ap: (lambda k: ap[:, 128 * (k % 4) + 64 * (k // 4):128 * (k % 4) + 64 * (k // 4) + 64])
                    gather(p0)
                    turn_gates(p0)
                    turn(p0)
                    pe.wait_ge(zeroed, r + 1 + START)
                    pe.sem_inc(aloneT, 1)
                    with pe.Fori(0, BODIES) as it:
                        for j in range(PER_BODY):
                            e = e0 + (it * PER_BODY + j)
                            m0 = p0 + (it * PER_BODY + j)
                            m = p0 + (it * PER_BODY + (j + 1))

                            def scatter_before(b, e=e, m0=m0, j=j):
                                if b == 0:
                                    pe.wait_ge(yEvac, e + START)
                                    pe.wait_ge(gtOut, m0 + START)
                                scatter(b, m0, (j + 1) % 2)

                            pe.wait_ge(ehDone, m + START)
                            pe.wait_ge(xgTOut, m + START)
                            pe.wait_ge(aDone, e + START)
                            product(0, 0, half_c(xgT), e, it, j, [lambda b=b: scatter_before(b) for b in range(3)])
                            pe.wait_ge(uDone, e + START)
                            product(1, 1, half_c(xgT), e, it, j)
                            gather(m)
                            turn_gates(m)
                            pe.wait_ge(hidDone, e + 1 + START)
                            pe.wait_ge(hidTOut, e + START)
                            for c in range(4):
                                ins = TR(ps[:, 4, 128 * c:128 * c + 128], hid[:, 128 * c:128 * c + 128], ident)
                            ins.then_inc(hidTMM, 1)
                            turn(m)
                            pe.wait_ge(hidTOut, e + 1 + START)
                            pe.wait_ge(yEvac, e + START)
                            product(2, 2, half_c(hidT), e, it, j)
                    pe.wait_ge(yEvac, e0 + E + START)
                    for b in range(3):
                        scatter(b, p0 + E, 1)
                    pe.nop()
                with pe.Else():
                    pe.nop()


_IN = ["x_prompt", "x_sample", "state_conv", "state_hgrn", "w_in", "w_out", "router_w", "router_b", "w_gate", "b_gate",
       "w_up", "b_up", "w_down", "b_down", "final_norm_w"]
_ROWS = ["lb_logits", "conv_w", "conv_b", "gnorm_w", "norm_mix_w", "norm_ffn_w"]
_OUT = [("y_prompt", (1, 256, 1024)), ("y_sample", (8, 8, 1024)), ("new_conv_prompt", (1, 1, 2, 512)),
        ("new_hgrn_prompt", (1, 1, 4, 128, 128)), ("new_conv_sample", (1, 8, 2, 512)),
        ("new_hgrn_sample", (1, 8, 4, 128, 128))]


def _constants():
    import numpy as np
    p = np.arange(128)
    slots = np.tile(np.arange(1, 65), 2)
    pick = (p[:, None] % 32 == np.arange(34)[None]) & (p[:, None] // 32 != 1)
    parts = [np.eye(128), p[:, None] < p[None], np.ones((128, 128)), np.broadcast_to(slots, (128, 128)), pick,
             np.broadcast_to(64 * np.arange(8), (128, 8)), p[:, None] // 8 == np.arange(8)[None],
             np.broadcast_to(np.arange(32), (128, 32))]
    consts = np.ascontiguousarray(np.concatenate([a.astype(np.float32) for a in parts], axis=1))
    s, t = p[:, None], p[None]
    lev = [(s // (2 * n) == t // (2 * n)) & (s // n % 2 == 0) & (t // n % 2 == 1) for n in (1, 2, 4, 8, 16, 32, 64)]
    return consts, np.ascontiguousarray(np.stack(lev, axis=1).astype(np.float32))


def kernel(**inputs):
    import numpy as np
    import concourse.bacc as bacc
    from concourse.bass_utils import run_bass_kernel_spmd

    nc = bacc.Bacc("TRN2", target_bir_lowering=False, num_devices=1)
    arrays = {n: np.ascontiguousarray(inputs[n]) for n in _IN}
    for n in _ROWS:
        arrays[n] = np.ascontiguousarray(inputs[n]).reshape(-1, 128)
    arrays["consts"], arrays["lev_mask"] = _constants()
    aps = {n: nc.dram_tensor("in_" + n, a.shape, mybir.dt.from_np(a.dtype), kind="ExternalInput").ap()
           for n, a in arrays.items()}
    for n, shape in _OUT:
        aps[n] = nc.dram_tensor(n, shape, mybir.dt.float32, kind="ExternalOutput").ap()
    hybrid_shortconv_hgrn2_moe_step(nc, aps)
    r = run_bass_kernel_spmd(nc, [{"in_" + n: a for n, a in arrays.items()}], core_ids=[0])
    return tuple(r.results[0][n] for n, _ in _OUT)
```

```python
import concourse.bass as bass
from concourse import mybir
from contextlib import ExitStack


def hybrid_shortconv_hgrn2_moe_step(nc, A):
    f32, bf16, u8 = mybir.dt.float32, mybir.dt.bfloat16, mybir.dt.uint8
    i32, u32 = mybir.dt.int32, mybir.dt.uint32
    ALU, ACT, AX = mybir.AluOpType, mybir.ActivationFunctionType, mybir.AxisListType

    D = 1024
    KT = D // 128
    NP, NSEQ, LS = 256, 8, 8
    NT = NP + NSEQ * LS
    TOK = [(0, 128), (128, 128), (256, 64)]
    NH = 4
    E = 32
    SLOTS = 64
    ROUNDS = NT // SLOTS
    TOPK = 4
    LIMIT, ALPHA, EPS = 7.0, 1.702, 1e-6
    NLEV = 7

    NR = 16
    W_CHUNK = {"f": (2, 8), "q": (4, 6), "i": (6, 10), "g": (8, 12), "cg": (10, 2), "vc": (12, 4), "bg": (14, 0)}
    L_S0, L_BIAS, L_WOUT, L_EXP = 0, 18, 20, 24
    LPE = 12
    PER_BODY = 4
    BODIES = E // PER_BODY

    def ring_value(L):
        special = (L_S0, L_S0 + 1, L_S0 + NR, L_S0 + NR + 1, L_BIAS, L_BIAS + 1)
        return 16 * sum(1 for q in range(L % NR, L + 1, NR) if q not in special)

    UNITS = ([("f", h) for h in range(NH)] + [("q", h) for h in range(NH)]
             + [("i", c, b) for c in range(2) for b in range(2)] + [("i", 0, 2)] + [("g", h) for h in range(NH)]
             + [("cg", c) for c in range(NH)] + [("vc", c) for c in range(NH)] + [("bg", c) for c in range(NH)])
    UIDX = {u: n for n, u in enumerate(UNITS)}
    UNITS_OF = [(len(UNITS) + 1) // 2, len(UNITS) // 2]
    STEPS = ([("lev", l, p) for l in range(NLEV + 1) for p in range(2)] + [("cross",)] + [("o", h) for h in range(NH)]
             + [("ss", h) for h in range(NH)] + [("ktok",), ("pause",), ("stp",)] + [("sts", h) for h in range(NH)])
    SCHED = []
    left = list(STEPS)
    for n, u in enumerate(UNITS):
        SCHED.append(u)
        for _ in range(int(n == 6) if n < 8 else 1 + n % 2):
            if left:
                SCHED.append(left.pop(0))
    SCHED += left

    LGB = [5, 0, 1]

    def load_done(L):
        for kind, (l0, _) in W_CHUNK.items():
            if l0 <= L < l0 + 2:
                return 1 + (UIDX[(kind, 0, 2)] if kind == "i" else UIDX[(kind, 2 * (L - l0) + 1)])

    ctx = ExitStack()
    with ctx:
        def sb(name, shape, dt=f32):
            return ctx.enter_context(nc.sbuf_tensor(name, shape, dt))

        def sem(name):
            return ctx.enter_context(nc.semaphore(name))

        ring = sb("ring", [128, NR, 2048])
        x = sb("x", [128, 3, D])
        R1 = sb("R1", [128, 5120])
        R2 = sb("R2", [128, 2560])
        R3 = sb("R3", [128, 4608])
        R4 = sb("R4", [128, 2632])

        def view(region, at, pattern=None, **kw):
            n = 1
            for v in kw.pop("shape"):
                n *= v
            ap = region[:, at:at + n]
            return ap.rearrange(pattern, **kw) if pattern else ap

        hT = view(R1, 0, "p (k t) -> p k t", shape=(8, NT), k=8)
        qP = view(R1, 2560, "p (h t) -> p h t", shape=(4, NT), h=4)
        kS = view(R1, 3840, "p (h t) -> p h t", shape=(4, NT), h=4)
        vSel = [view(R1, at, "p (b d) -> p b d", shape=(8, 128), b=8) for at in (2560, 3584)]
        h2p = R1[:, 0:4608].bitcast(bf16).rearrange("p (s b d) -> p s b d", s=3, b=3)
        yout = view(R1, 0, "p (b d) -> p b d", shape=(3, D), b=3)
        junk2 = view(R1, 3072, shape=(D,))
        mixT = view(R2, 0, "p (k t) -> p k t", shape=(8, NT), k=8)
        fdec = view(R2, 0, "p (h t) -> p h t", shape=(4, NT), h=4)
        q = view(R2, 1280, "p (h t) -> p h t", shape=(4, NT), h=4)
        fnw = view(R2, 0, shape=(D,))
        g = view(R3, 0, "p (h t) -> p h t", shape=(4, NT), h=4)
        sc = view(R3, 1280, "p (h t) -> p h t", shape=(4, 448), h=4)
        v = view(R3, 3072, "p (b d) -> p b d", shape=(3, 512), b=3)
        rowScale = view(R3, 0, "p (b t) -> p b t", shape=(3, 128), b=3)
        histRows = view(R3, 3072, shape=(512,))
        maskIn = view(R3, 3584, "p (l t) -> p l t", shape=(NLEV, 128), l=NLEV)
        h2f = view(R3, 0, "p (b d) -> p b d", shape=(2, D), b=2)
        kTok = view(R3, 1280, "p (n d) -> p n d", shape=(12, 128), n=12)
        stP = view(R3, 0, "p (h d) -> p h d", shape=(4, 128), h=4)
        tailT = view(R3, 2560, shape=(512,))
        x2T = view(R3, 3072, "p (k t) -> p k t", shape=(8, 128), k=8)
        ga, gs, gu, gt, xgs, xgT, hidT, ysb, hid = [view(R3, 512 * n, shape=(512,)) for n in range(9)]
        cv = view(R4, 0, "p (c t) -> p c t", shape=(4, NT), c=4)
        u = view(R4, 1280, "p (c t) -> p c t", shape=(4, NT + 2 + 2 * NSEQ), c=4)
        junk = view(R4, 0, shape=(D,))
        bias3 = R4[:, 0:1536].bitcast(bf16).rearrange("p (m d) -> p m d", m=3)
        G = view(R4, 1536, "p (b s) -> p b s", shape=(3, 128), b=3)
        oh = view(R4, 1536, "p (b k e) -> p b k e", shape=(3, TOPK, E), b=3, k=TOPK)
        GT = view(R4, 1920, "p (n t) -> p n t", shape=(2, NT), n=2)

        consts = sb("consts", [128, 128 * 4 + 34 + 8 + 8 + 32])
        ident, tri, ones, iota2 = [consts[:, 128 * n:128 * n + 128] for n in range(4)]
        expCol = consts[:, 512:546]
        roundStart = consts[:, 546:554]
        seqMask = consts[:, 554:562]
        expId = consts[:, 562:594]
        levMask = sb("levMask", [128, NLEV, 128], u8)
        trib = sb("trib", [128, 128], bf16)
        onesb = sb("onesb", [128, 128], bf16)
        rw = sb("rw", [128, 8, E])
        rb = sb("rb", [128, E])
        parRows = sb("parRows", [44, 128])
        par = sb("par", [128, 44])
        lbW = sb("lbW", [128, 5, 4])
        lb = sb("lb", [128, 4])
        oml = sb("oml", [128, 4])
        epsT = sb("epsT", [128, 1])
        tail = sb("tail", [128, 4, 18])
        st = sb("st", [128, 24])
        f8 = sb("f8", [128, 4, NSEQ])
        lg = sb("lg", [128, 3, E])
        mx = sb("mx", [128, 3, 8])
        mi = sb("mi", [128, 3, 8], u32)
        mif = sb("mif", [128, 3, 8])
        ex = sb("ex", [128, 3, 4])
        comb = sb("comb", [128, 3, E + 1])
        sel = sb("sel", [128, 3, E], bf16)
        posm = sb("posm", [128, 3, E + 1])
        cmax = sb("cmax", [128, 1])
        roundsT = sb("rounds", [128, 1], i32)
        P = sb("P", [128, 3, SLOTS], bf16)
        eh = sb("eh", [128, 2, SLOTS], bf16)

        ps = ctx.enter_context(nc.psum_tensor("ps", [128, 8, 512], f32))

        ringIn = [sem(f"ring_in{s}") for s in range(NR)]
        xIn = [sem(f"x_in{b}") for b in range(3)]
        constIn, maskInSem, parIn, routerIn, histIn = sem("const_in"), sem("mask_in"), sem("par_in"), sem("router_in"), sem("hist_in")
        s0In, biasIn, fnwIn = sem("s0_in"), sem("bias_in"), sem("fnw_in")
        s0Out, stOut, tailOut, yOut = sem("s0_out"), sem("state_out"), sem("tail_out"), sem("y_out")
        parMM, histMM, xTMM, projMM, levMM, oMM = sem("par_mm"), sem("hist_mm"), sem("xT_mm"), sem("proj_mm"), sem("lev_mm"), sem("o_mm")
        ssMM, kTokMM, stPMM, stSMM, tailMM = sem("ss_mm"), sem("ktok_mm"), sem("stp_mm"), sem("sts_mm"), sem("tail_mm")
        woutMM, x2TMM, lgMM, posMM = sem("wout_mm"), sem("x2T_mm"), sem("lg_mm"), sem("pos_mm")
        wUsed = sem("w_used")
        xgMM, gtMM, xgTMM, hidTMM, scatMM = sem("xg_mm"), sem("gt_mm"), sem("xgT_mm"), sem("hidT_mm"), sem("scat_mm")
        unitOut = [sem(f"unit_out{n}") for n in range(2)]
        ssqDone, rootDone, expDone = sem("ssq_done"), sem("root_done"), sem("lbexp_done")
        gSig, crossOut, oSq, oRoot = sem("gsig"), sem("cross_out"), sem("osq"), sem("oroot")
        kTokOut, tailTOut = sem("ktok_out"), sem("tailT_out")
        ssq2Done, root2Done, x2TOut, exDone, partDone = (sem("ssq2"), sem("root2"), sem("x2T_out"), sem("ex_done"),
                                                          sem("part_done"))
        sigDone, xgOut, gtOut, hidTOut, yEvac = sem("sig_done"), sem("xg_out"), sem("gt_out"), sem("hidT_out"), sem("y_evac")
        finSq, finRoot = sem("fin_sq"), sem("fin_root")
        step = sem("dve_step")
        parOut, scaleDone, hTOut, levOut, kScaled = sem("par_out"), sem("scale_done"), sem("hT_out"), sem("lev_out"), sem("k_scaled")
        f8Out, mixDone, stPOut, stSOut = sem("f8_out"), sem("mix_done"), sem("stp_out"), sem("sts_out")
        x2Done, resid, mxDone, selDone, posOut = (sem("x2_done"), sem("resid"), sem("mx_done"),
                                                         sem("sel_done"), sem("pos_out"))
        h2Parts, roundsDone, histOut, epsOut, maskOut = (sem("h2_parts"), sem("rounds_done"), sem("hist_out"), sem("eps_out"),
                                                         sem("mask_out"))
        prep, prepG, aDone, uDone, tDone = sem("prep"), sem("prep_gates"), sem("a_done"), sem("u_done"), sem("t_done")
        hidDone, xgTOut, accDone = sem("hid_done"), sem("xgT_out"), sem("acc_done")
        posShift, zeroed, moeDone, finDone, normed = sem("pos_shift"), sem("zeroed"), sem("moe_done"), sem("fin_done"), sem("normed")
        lastMM = sem("last_mm")
        aloneP, aloneV, aloneT = sem("alone_pool"), sem("alone_dve"), sem("alone_pe")
        warm = sem("warm")
        vSelDone, s0Scaled, tailIn, biasDone, biasPart, biasRest, ehDone = (sem("vsel_done"), sem("s0_scaled"), sem("tail_in"),
                                                                  sem("bias_done"), sem("bias_part"), sem("bias_rest"), sem("eh_done"))

        w_in = A["w_in"][0].rearrange("(k p) n -> p k n", p=128)
        w_out = A["w_out"][0].rearrange("(k p) n -> p k n", p=128)
        w_exp = [A[n][0].rearrange("e (k p) n -> e p k n", p=128) for n in ("w_gate", "w_up", "w_down")]
        b_exp = [A[n][0] for n in ("b_gate", "b_up", "b_down")]
        s0 = ring[:, L_S0:L_S0 + 2, :].rearrange("p s (n d) -> p (s n) d", d=128)
        s0v = s0.rearrange("p (b h) d -> p b h d", h=NH)
        biasRaw = ring[:, L_BIAS % NR:L_BIAS % NR + 2, :].rearrange("p s n -> p (s n)")

        def slot_k(L, cols):
            return ring[:, L % NR, :].rearrange("p (k n) -> p k n", n=cols)

        def later_blocks(ap, l):
            lead = " ".join("abc"[:len(ap.shape) - 1])
            v = ap.rearrange(f"{lead} (n two t) -> {lead} n two t", two=2, t=1 << (l - 1))
            return v[:, :, 1, :] if len(ap.shape) == 2 else v[:, :, :, 1, :]

        START = 1

        def credit(eng, *sems):
            for s in sems:
                eng.sem_inc(s, START)

        def further_rounds(eng, one_round):
            rounds = eng.value_load(roundsT[0:1, :], min_val=1, max_val=ROUNDS)
            with eng.If(rounds > 1):
                with eng.Fori(1, ROUNDS) as r:
                    with eng.If(rounds > r):
                        one_round(r)
                        eng.nop()
                    with eng.Else():
                        eng.nop()
                eng.nop()
            with eng.Else():
                eng.nop()

        block = ctx.enter_context(nc.Block())

        @block.sync
        def _(sp):
            def load_expert(e, j, s):
                m, c = divmod(j, 4)
                sp.dma_start(ring[:, s, :].rearrange("p (k n) -> p k n", n=D),
                             w_exp[m][e, :, 2 * c:2 * c + 2, :]).then_inc(ringIn[s], 16)

            def load_in(L, col):
                sp.dma_start(slot_k(L, 256), w_in[:, :, 256 * col:256 * col + 256]).then_inc(ringIn[L % NR], 16)

            sp.dma_start(consts[:], A["consts"]).then_inc(constIn, 16)
            for b, (t0, n) in enumerate(TOK):
                src = A["x_prompt"][0, t0:t0 + n, :] if b < 2 else A["x_sample"].rearrange("s t d -> (s t) d")
                sp.dma_start(x[0:n, b, :], src).then_inc(xIn[b], 16)
            for kind in ("f", "q", "i", "g"):
                for j in range(2):
                    load_in(W_CHUNK[kind][0] + j, W_CHUNK[kind][1] + j)
            sp.dma_start(s0, A["state_hgrn"][0].rearrange("b h k v -> k (b h) v")).then_inc(s0In, 16)
            for kind in ("cg", "vc", "bg"):
                for j in range(2):
                    load_in(W_CHUNK[kind][0] + j, W_CHUNK[kind][1] + j)
            sp.wait_ge(projMM, load_done(L_BIAS + 1 - NR))
            for m in range(3):
                for part in range(4):
                    sp.dma_start(biasRaw[32 * part:32 * part + 32, D * m:D * m + D], b_exp[m]).then_inc(biasIn, 16)
            for c in range(4):
                sp.wait_ge(projMM, load_done(L_WOUT + c - NR))
                sp.dma_start(slot_k(L_WOUT + c, D), w_out[:, 2 * c:2 * c + 2, :]).then_inc(ringIn[(L_WOUT + c) % NR], 16)
            for n in range(LPE * PER_BODY):
                L = L_EXP + n
                before = L - NR
                if before in (L_S0 + NR, L_S0 + NR + 1):
                    sp.wait_ge(s0Out, 16)
                elif before in (L_BIAS, L_BIAS + 1):
                    sp.wait_ge(biasDone, 1)
                elif before < NR:
                    sp.wait_ge(projMM, load_done(before))
                elif before < L_EXP:
                    sp.wait_ge(woutMM, 3)
                else:
                    sp.wait_ge(wUsed, n - NR + 1 + START)
                load_expert(n // LPE, n % LPE, L % NR)

            def body(first, it):
                for n in range(LPE * PER_BODY):
                    sp.wait_ge(wUsed, (first + (n - NR + 1)) + it * (LPE * PER_BODY) + START)
                    load_expert(it * PER_BODY + n // LPE, n % LPE, (L_EXP + n) % NR)

            with sp.Fori(1, BODIES) as it:
                body(0, it)
            sp.wait_ge(roundsDone, 1)
            def all_loads(r):
                with sp.Fori(0, BODIES) as it:
                    body(r * (LPE * E), it)

            further_rounds(sp, all_loads)
            yp = A["y_prompt"][0].rearrange("(b p) d -> b p d", p=128)
            for b, (t0, n) in enumerate(TOK):
                sp.wait_ge(finDone, b + 1)
                dst = yp[b] if b < 2 else A["y_sample"].rearrange("s t d -> (s t) d")
                sp.dma_start(dst, yout[0:n, b, :]).then_inc(yOut, 16)
            sp.wait_ge(yOut, 48)
            sp.wait_ge(s0Out, 16)
            sp.wait_ge(stOut, 16)
            sp.wait_ge(tailOut, 32)

        @block.gpsimd
        def _(pool):
            credit(pool, ehDone)
            pool.dma_start(rw[:], A["router_w"][0].rearrange("(k p) e -> p k e", p=128)).then_inc(routerIn, 16)
            pool.dma_start(rb[:], A["router_b"][0].partition_broadcast(128)).then_inc(routerIn, 16)
            for h in range(NH):
                if h == 0:
                    pool.wait_ge(oMM, NH)
                    pool.wait_ge(f8Out, 1)
                if h == 1:
                    pool.wait_ge(kTokMM, 1)
                if h >= 2:
                    pool.wait_ge(stSMM, h - 1)
                pool.tensor_tensor(vSel[h % 2][0:64], v[0:64, 2, 128 * h:128 * h + 128].unsqueeze(1).broadcast_to([64, 8, 128]),
                                   seqMask[0:64, :].unsqueeze(2).broadcast_to([64, 8, 128]), ALU.mult).then_inc(vSelDone, 1)
                pool.tensor_tensor(s0v[:, :, h, :], s0v[:, :, h, :], f8[:, h, :].unsqueeze(2).broadcast_to([128, 8, 128]),
                                   ALU.mult).then_inc(s0Scaled, 1)
            pool.wait_ge(stSOut, NH)
            pool.dma_start(A["new_hgrn_sample"][0].rearrange("b h k v -> k (b h) v"), s0).then_inc(s0Out, 16)
            for n in range(2):
                pool.wait_ge(unitOut[n], UNITS_OF[n])
            pool.tensor_copy(tail[:, :, 0:2], u[:, :, NP:NP + 2])
            pool.tensor_copy(tail[:, :, 2:18].rearrange("p c (s w) -> p c s w", w=2),
                             u[:, :, NP + 2:].rearrange("p c (s w) -> p c s w", w=10)[:, :, :, 8:10]).then_inc(tailIn, 1)

            for b in (1, 2):
                n = TOK[b][1]
                hf = h2f[0:n, b % 2, :]
                pool.wait_ge(partDone, 2 * b + 1)
                pool.wait_ge(normed, b + 1)
                pool.tensor_tensor(hf, hf, h2p[0:n, 0, b, :], ALU.subtract).then_inc(resid, 1)
                pool.wait_ge(partDone, 2 * b + 2)
                pool.wait_ge(resid, b + 1)
                pool.tensor_tensor(h2p[0:n, 2, b, :], hf, h2p[0:n, 1, b, :], ALU.subtract).then_inc(h2Parts, 1)

            pool.wait_ge(woutMM, 3)
            pool.dma_start(fnw, A["final_norm_w"].partition_broadcast(128)).then_inc(fnwIn, 16)

            def pick(value, par):
                pool.sem_inc(aloneP, 1)
                pool.tensor_copy(eh[:, par, :], expCol[:, value].broadcast_to([128, SLOTS])).then_inc(ehDone, 1)

            pool.wait_ge(tailIn, 1)
            def one_round(r):
                pool.wait_ge(ehDone, r * (E + 1) + START)
                pool.wait_ge(wUsed, r * (LPE * E) + START)
                pick(slice(0, 1), 0)
                with pool.Fori(0, BODIES) as it:
                    for j in range(PER_BODY):
                        pool.wait_ge(wUsed, r * (LPE * E) + (it * (LPE * PER_BODY) + LPE * j) + START)
                        pick(bass.ds(it * PER_BODY + (j + 1), 1), (j + 1) % 2)

            one_round(0)
            pool.wait_ge(roundsDone, 1)
            further_rounds(pool, one_round)

        @block.scalar
        def _(act):
            credit(act, sigDone, xgOut, gtOut, hidTOut, yEvac)
            act.dma_start(parRows[:], A["par_rows"]).then_inc(parIn, 16)
            act.dma_start(histRows[0:16, :], A["state_conv"][0].rearrange("b w c -> (b w) c")).then_inc(histIn, 16)
            act.dma_start(maskIn, A["lev_mask"]).then_inc(maskInSem, 16)
            act.wait_ge(epsOut, 1)
            act.activation(st[:, 22:23], epsT[:], ACT.Sqrt).then_inc(warm, 1)
            for b, (t0, n) in enumerate(TOK):
                act.wait_ge(xIn[b], 16)
                if b:
                    act.wait_ge(ssqDone, b)
                act.activation(junk[0:n], x[0:n, b, :], ACT.Square, accum_out=st[0:n, b:b + 1]).then_inc(ssqDone, 1)
                act.wait_ge(ssqDone, b + 1)
                act.activation(st[0:n, 3 + b:4 + b], st[0:n, b:b + 1], ACT.Sqrt, bias=epsT[0:n, :], scale=1.0 / D)\
                   .then_inc(rootDone, 1)
            act.wait_ge(parOut, 2)
            act.activation(lbW[:, 1:3, :], lbW[:, 1:3, :], ACT.Exp).then_inc(expDone, 1)
            for item in SCHED:
                kind = item[0]
                if kind in ("f", "q", "i", "g", "cg"):
                    n = UIDX[item]
                    src = ps[:, n % 2, 0:NT]
                    act.wait_ge(projMM, n + 1)
                    out = unitOut[n % 2]
                if kind == "f":
                    h = item[1]
                    act.activation(fdec[:, h, :], src, ACT.Sigmoid)
                    act.activation(kS[:, h, :], src, ACT.Sigmoid, scale=-1.0).then_inc(out, 1)
                elif kind == "q":
                    act.activation(q[:, item[1], :], src, ACT.Copy).then_inc(out, 1)
                elif kind == "i":
                    _, c, b = item
                    act.wait_ge(maskOut, 1)
                    if b < 2:
                        act.activation(v[:, b, 256 * c:256 * c + 256], ps[:, n % 2, 0:256], ACT.Copy).then_inc(out, 1)
                    else:
                        act.activation(v[0:64, 2, 0:256], ps[0:64, n % 2, 0:256], ACT.Copy)
                        act.activation(v[0:64, 2, 256:512], ps[64:128, n % 2, 0:256], ACT.Copy).then_inc(out, 1)
                elif kind == "g":
                    act.activation(g[:, item[1], :], src, ACT.Sigmoid).then_inc(gSig, 1)
                elif kind == "cg":
                    act.activation(cv[:, item[1], :], src, ACT.Copy).then_inc(out, 1)
                elif kind == "cross":
                    act.wait_ge(levMM, 2 * (NLEV + 1) + 1)
                    act.activation(sc[:, :, 256:384], ps[:, 6, :].rearrange("p (h t) -> p h t", h=4), ACT.Copy)\
                       .then_inc(crossOut, 1)
                elif kind == "o":
                    h = item[1]
                    act.wait_ge(oMM, h + 1)
                    act.activation(sc[:, h, 0:NT], ps[:, 2 + h, 0:NT], ACT.Square).then_inc(oSq, 1)
                elif kind == "ss":
                    h = item[1]
                    act.wait_ge(ssMM, h + 1)
                    act.activation(sc[:, h, 0:NT], ps[:, 6 + h % 2, 0:NT], ACT.Sqrt, bias=epsT[:], scale=1.0 / 128).then_inc(oRoot, 1)
                elif kind == "ktok":
                    act.wait_ge(kTokMM, 1)
                    act.wait_ge(mixDone, NH)
                    act.activation(kTok[:, 0:8, :].rearrange("p n d -> p (n d)"), ps[:, 6:8, :].rearrange("p a n -> p (a n)"),
                                   ACT.Copy)
                    act.activation(kTok[0:64, 8:12, :].rearrange("p n d -> p (n d)"), ps[0:64, 2, :], ACT.Copy).then_inc(kTokOut, 1)
                elif kind == "stp":
                    act.wait_ge(stPMM, 1)
                    act.activation(stP.rearrange("p h d -> p (h d)"), ps[:, 3, :], ACT.Copy).then_inc(stPOut, 1)
            act.wait_ge(stPOut, 1)
            act.dma_start(A["new_hgrn_prompt"][0, 0].rearrange("h k v -> k h v"), stP).then_inc(stOut, 16)
            b3 = bias3.rearrange("p m d -> p (m d)")
            act.wait_ge(biasIn, 16 * 12)
            act.wait_ge(tailIn, 1)
            act.activation(b3, biasRaw[:, 0:3 * D], ACT.Copy).then_inc(biasPart, 1)
            act.wait_ge(biasRest, 1)
            act.activation(b3[64:128], biasRaw[64:128, 0:3 * D], ACT.Copy).then_inc(biasPart, 1)
            act.wait_ge(biasRest, 2)
            act.activation(b3[96:128], biasRaw[96:128, 0:3 * D], ACT.Copy).then_inc(biasDone, 1)
            act.wait_ge(tailMM, 1)
            act.activation(tailT[0:18, :], ps[0:18, 7, :], ACT.Copy).then_inc(tailTOut, 1)
            act.wait_ge(tailTOut, 1)
            act.dma_start(A["new_conv_prompt"][0, 0], tailT[0:2, :]).then_inc(tailOut, 16)
            act.dma_start(A["new_conv_sample"][0].rearrange("b w c -> (b w) c"), tailT[2:18, :]).then_inc(tailOut, 16)

            act.wait_ge(stOut, 16)

            def root2(b):
                t0, n = TOK[b]
                act.wait_ge(x2Done, b + 1)
                if b == 2:
                    act.wait_ge(h2Parts, 1)
                act.activation(h2f[0:n, b % 2, :], x[0:n, b, :], ACT.Square, accum_out=st[0:n, 9 + b:10 + b]).then_inc(ssq2Done, 1)
                act.wait_ge(ssq2Done, b + 1)
                act.activation(st[0:n, 12 + b:13 + b], st[0:n, 9 + b:10 + b], ACT.Sqrt, bias=epsT[0:n, :], scale=1.0 / D)\
                   .then_inc(root2Done, 1)

            def part(b, p):
                n = TOK[b][1]
                act.wait_ge(resid if p else normed, b + 1)
                act.activation(h2p[0:n, p, b, :], h2f[0:n, b % 2, :], ACT.Copy).then_inc(partDone, 1)

            def exps(b):
                act.wait_ge(mxDone, b + 1)
                act.activation(ex[:, b, :], lg[:, b, 0:4], ACT.Exp).then_inc(exDone, 1)

            def bring_table(func, n):
                act.wait_ge(warm, n)
                act.activation(st[:, 22:23], epsT[:], func).then_inc(warm, 1)

            bring_table(ACT.Sqrt, 1)
            root2(0)
            part(0, 0)
            part(0, 1)
            root2(1)
            exps(0)
            part(1, 0)
            bring_table(ACT.Sqrt, 2)
            root2(2)
            part(1, 1)
            exps(1)
            part(2, 0)
            exps(2)
            part(2, 1)
            bring_table(ACT.Sigmoid, 3)
            act.wait_ge(tailOut, 32)
            def one_round(r):
                p0, e0 = r * (E + 1), r * E

                def prefetch(m, scattered, par):
                    act.wait_ge(xgMM, m + 1 + START)
                    act.wait_ge(xgTMM, m + START)
                    act.activation(xgs, ps[:, 3, :], ACT.Copy).then_inc(xgOut, 1)
                    act.wait_ge(gtMM, m + 1 + START)
                    act.wait_ge(scatMM, scattered + START)
                    act.activation(GT[:, par, :], ps[:, 5, 0:NT], ACT.Copy).then_inc(gtOut, 1)

                prefetch(p0, e0 * 3, 0)
                with act.Fori(0, BODIES) as it:
                    for j in range(PER_BODY):
                        e = e0 + (it * PER_BODY + j)
                        m = p0 + (it * PER_BODY + (j + 1))
                        act.wait_ge(aDone, e + 1 + START)
                        act.wait_ge(hidDone, e + START)
                        act.activation(gs, ga, ACT.Sigmoid, scale=ALPHA).then_inc(sigDone, 1)
                        prefetch(m, e * 3 + 3, (j + 1) % 2)
                        act.wait_ge(hidTMM, e + 1 + START)
                        act.wait_ge(wUsed, e * LPE + START)
                        act.activation(hidT, ps[:, 4, :], ACT.Copy).then_inc(hidTOut, 1)
                        act.wait_ge(wUsed, e * LPE + LPE + START)
                        act.wait_ge(scatMM, e * 3 + 3 + START)
                        act.activation(ysb, ps[:, 2, :], ACT.Copy).then_inc(yEvac, 1)

            one_round(0)
            act.wait_ge(roundsDone, 1)
            further_rounds(act, one_round)
            bring_table(ACT.Sqrt, 4)
            for b, (t0, n) in enumerate(TOK):
                act.wait_ge(moeDone, b + 1)
                if b:
                    act.wait_ge(finSq, b)
                act.activation(junk2[0:n], x[0:n, b, :], ACT.Square, accum_out=st[0:n, b:b + 1]).then_inc(finSq, 1)
                act.wait_ge(finSq, b + 1)
                act.activation(st[0:n, 3 + b:4 + b], st[0:n, b:b + 1], ACT.Sqrt, bias=epsT[0:n, :], scale=1.0 / D)\
                   .then_inc(finRoot, 1)

        @block.vector
        def _(dve):
            count = {}

            def did(ins, s=step):
                ins.then_inc(s, 1)
                count[s.name] = count.get(s.name, 0) + 1
                return s, count[s.name]

            def need(*done):
                for s, n in done:
                    dve.wait_ge(s, n)

            credit(dve, posShift, prep, prepG, aDone, uDone, tDone, hidDone, xgTOut, accDone)
            TT, TS, STT = dve.tensor_tensor, dve.tensor_scalar, dve.scalar_tensor_tensor
            did(dve.memset(epsT[:], EPS), epsOut)
            did(dve.memset(u[:, :, 0:2], 0.0))
            did(dve.memset(comb[:], 0.0))
            did(dve.memset(posm[:], 0.0))
            did(dve.memset(lg[:], 0.0))
            did(dve.memset(mif[:], 0.0))
            dve.wait_ge(constIn, 16)
            for b, (t0, n) in enumerate(TOK):
                dve.wait_ge(rootDone, b + 1)
                need(did(dve.reciprocal(st[0:n, 6 + b:7 + b], st[0:n, 3 + b:4 + b])))
                TS(rowScale[0:n, b, :], ident[0:n, :], st[0:n, 6 + b:7 + b], None, ALU.mult).then_inc(scaleDone, 1)
            dve.wait_ge(parMM, 1)
            need(did(dve.tensor_copy(par[:], ps[:, 0, 0:44]), parOut))
            LB, CW, CB, GN, NM, NF = 0, 8, 20, 24, 28, 36
            need(did(TT(lbW[:, 0, :], par[:, LB:LB + 4], par[:, LB + 4:LB + 8], ALU.max)))
            did(TT(lbW[:, 1:3, :], par[:, LB:LB + 8].rearrange("p (a h) -> p a h", a=2),
                   lbW[:, 0, :].unsqueeze(1).broadcast_to([128, 2, 4]), ALU.subtract), parOut)
            for b, (t0, n) in enumerate(TOK):
                dve.wait_ge(xTMM, b + 1)
                TT(hT[:, :, t0:t0 + n], ps[:, 2 + 2 * b:4 + 2 * b, :].rearrange("p a (k t) -> p (a k) t", t=128)[:, :, 0:n],
                   par[:, NM:NM + 8].unsqueeze(2).broadcast_to([128, 8, n]), ALU.mult).then_inc(hTOut, 1)
            dve.wait_ge(histMM, 1)
            did(dve.tensor_copy(u[:, :, NP + 2:].rearrange("p c (s w) -> p c s w", w=10)[:, :, :, 0:2],
                                ps[:, 1, 0:64].rearrange("p (c s w) -> p c s w", c=4, w=2)), histOut)
            dve.wait_ge(expDone, 1)
            need(did(TT(lbW[:, 3, :], lbW[:, 1, :], lbW[:, 2, :], ALU.add)))
            need(did(dve.reciprocal(lbW[:, 4, :], lbW[:, 3, :])))
            need(did(TT(lb[:], lbW[:, 1, :], lbW[:, 4, :], ALU.mult)))
            need(did(TS(oml[:], lb[:], -1.0, 1.0, ALU.mult, ALU.add)))
            did(dve.tensor_copy(trib[:], tri))
            did(dve.tensor_copy(onesb[:], ones))
            dve.wait_ge(maskInSem, 16)
            did(dve.tensor_copy(levMask[:], maskIn), maskOut)
            dve.wait_ge(routerIn, 32)
            did(TT(rw[:], rw[:], par[:, NF:NF + 8].unsqueeze(2).broadcast_to([128, 8, E]), ALU.mult))

            pairs = lambda ap, p: ap[:, 2 * p:2 * p + 2, :]
            kDone, gateDone, decayDone = {}, {}, {}
            for item in SCHED:
                kind = item[0]
                if kind in ("f", "g", "vc", "bg"):
                    n = UIDX[item]
                    src = ps[:, n % 2, :]
                if kind == "f":
                    h = item[1]
                    dve.wait_ge(unitOut[n % 2], n // 2 + 1)
                    did(TS(fdec[:, h, :], fdec[:, h, :], oml[:, h:h + 1], lb[:, h:h + 1], ALU.mult, ALU.add))
                    kDone[h] = did(TS(kS[:, h, :], kS[:, h, :], oml[:, h:h + 1], None, ALU.mult), kScaled)
                elif kind == "g":
                    h = item[1]
                    dve.wait_ge(gSig, h + 1)
                    gateDone[h] = did(STT(g[:, h, :], src[:, 0:NT], par[:, GN + h:GN + h + 1], g[:, h, :], ALU.mult, ALU.mult), unitOut[n % 2])
                elif kind == "vc":
                    c = item[1]
                    m = UIDX[("cg", c)]
                    dve.wait_ge(unitOut[m % 2], m // 2 + 1)
                    dve.wait_ge(projMM, n + 1)
                    us = u[:, c, NP + 2:].rearrange("p (s w) -> p s w", w=10)
                    did(TT(u[:, c, 2:NP + 2], src[:, 0:NP], cv[:, c, 0:NP], ALU.mult))
                    TT(us[:, :, 2:10], src[:, NP:NT].rearrange("p (s w) -> p s w", w=8),
                       cv[:, c, NP:NT].rearrange("p (s w) -> p s w", w=8), ALU.mult).then_inc(unitOut[n % 2], 1)
                elif kind == "bg":
                    c = item[1]
                    m = UIDX[("vc", c)]
                    dve.wait_ge(unitOut[m % 2], m // 2 + 1)
                    us = u[:, c, NP + 2:].rearrange("p (s w) -> p s w", w=10)
                    cp, cs = cv[:, c, 0:NP], cv[:, c, NP:NT].rearrange("p (s w) -> p s w", w=8)
                    w = lambda j: par[:, CW + 4 * j + c:CW + 4 * j + c + 1]
                    did(TS(cp, u[:, c, 0:NP], w(0), par[:, CB + c:CB + c + 1], ALU.mult, ALU.add))
                    done = did(TS(cs, us[:, :, 0:8], w(0), par[:, CB + c:CB + c + 1], ALU.mult, ALU.add))
                    for j in (1, 2):
                        need(done)
                        did(STT(cp, u[:, c, j:NP + j], w(j), cp, ALU.mult, ALU.add))
                        done = did(STT(cs, us[:, :, j:8 + j], w(j), cs, ALU.mult, ALU.add))
                    dve.wait_ge(projMM, n + 1)
                    need(done)
                    TT(mixT[:, c, :], src[:, 0:NT], cv[:, c, :], ALU.mult).then_inc(unitOut[n % 2], 1)
                elif kind == "lev":
                    _, l, p = item
                    dve.wait_ge(levMM, 2 * l + p + 1)
                    pb = ps[:, 2 + 2 * p:4 + 2 * p, :]
                    tiles = pb[:, :, 0:256].rearrange("p h (b t) -> p h b t", b=2)
                    smp = pb[0:64, :, 256:320]
                    outT = pairs(sc, p)[:, :, 0:256].rearrange("p h (b t) -> p h b t", b=2)
                    outS = pairs(sc, p)[0:64, :, 384:448]
                    if l == 0:
                        did(TT(outT, tiles, ident.unsqueeze(1).unsqueeze(1).broadcast_to([128, 2, 2, 128]), ALU.mult))
                        need(did(TT(outS, smp, ident[0:64, 0:64].unsqueeze(1).broadcast_to([64, 2, 64]), ALU.mult)))
                        mq = [UIDX[("q", 2 * p)], UIDX[("q", 2 * p + 1)]]
                        need(kDone[2 * p + 1])
                        for m in mq:
                            dve.wait_ge(unitOut[m % 2], m // 2 + 1)
                        decayDone[p] = did(TT(pairs(qP, p), pairs(q, p), pairs(fdec, p), ALU.mult), levOut)
                    else:
                        size = 1 << (l - 1)
                        for hh in range(2):
                            m_ = later_blocks(levMask[:, l - 1, :], l)
                            m_ = m_.unsqueeze(1).broadcast_to([128, 2] + list(m_.shape[1:]))
                            last = did(dve.copy_predicated(later_blocks(outT[:, hh], l), m_, later_blocks(tiles[:, hh], l)))
                        if l <= 3:
                            m_ = later_blocks(levMask[0:64, l - 1, 0:64], l)
                            m_ = m_.unsqueeze(1).broadcast_to([64, 2] + list(m_.shape[1:]))
                            last = did(dve.copy_predicated(later_blocks(outS, l), m_, later_blocks(smp, l)))
                        need(last, decayDone[p])
                        cols = NT if size <= 4 else NP
                        blk = lambda ap: pairs(ap, p)[:, :, 0:cols].rearrange("p h (b two t) -> p h b two t", two=2, t=size)
                        nb = cols // (2 * size)
                        fv, qv, kv = blk(fdec), blk(qP), blk(kS)
                        shape = [128, 2, nb, size]
                        did(TT(qv[:, :, :, 1, :], qv[:, :, :, 1, :], fv[:, :, :, 0, size - 1:size].broadcast_to(shape), ALU.mult))
                        need(did(TT(kv[:, :, :, 0, :], kv[:, :, :, 0, :], fv[:, :, :, 1, size - 1:size].broadcast_to(shape), ALU.mult)))
                        decayDone[p] = did(TT(fv[:, :, :, 1, size - 1], fv[:, :, :, 1, size - 1], fv[:, :, :, 0, size - 1], ALU.mult), levOut)
                        if l == 3 and p == 1:
                            need(decayDone[0], decayDone[1])
                            did(dve.tensor_copy(f8[:], fdec[:, :, NP + 7:NT:8]), f8Out)
                elif kind == "ss":
                    h = item[1]
                    dve.wait_ge(oRoot, h + 1)
                    need(gateDone[h], did(dve.reciprocal(sc[:, h, 0:NT], sc[:, h, 0:NT])))
                    need(did(TT(g[:, h, :], g[:, h, :], sc[:, h, 0:NT], ALU.mult)))
                    TT(mixT[:, NH + h, :], ps[:, 2 + h, 0:NT], g[:, h, :], ALU.mult).then_inc(mixDone, 1)
                elif kind == "sts":
                    h = item[1]
                    dve.wait_ge(stSMM, h + 1)
                    dve.wait_ge(s0Scaled, h + 1)
                    TT(s0v[:, :, h, :], s0v[:, :, h, :], ps[:, 4:6, :].rearrange("p a (b d) -> p (a b) d", d=128), ALU.add)\
                        .then_inc(stSOut, 1)
                elif kind == "cross":
                    dve.wait_ge(levMM, 2 * (NLEV + 1) + 1)
                    need(decayDone[0], decayDone[1])
                    did(TT(kS[:, :, 0:128], kS[:, :, 0:128], fdec[:, :, 255:256].broadcast_to([128, 4, 128]), ALU.mult), levOut)
            dve.wait_ge(biasPart, 1)
            b3 = bias3.rearrange("p m d -> p (m d)")
            TT(biasRaw[64:128, 0:3 * D], biasRaw[64:128, 0:3 * D], b3[64:128], ALU.subtract).then_inc(biasRest, 1)
            dve.wait_ge(biasPart, 2)
            dve.wait_ge(biasRest, 1)
            TT(biasRaw[96:128, 0:3 * D], biasRaw[96:128, 0:3 * D], b3[96:128], ALU.subtract).then_inc(biasRest, 1)

            WB = [0, 2, 4]

            def add_mixer(b):
                t0, n = TOK[b]
                dve.wait_ge(woutMM, b + 1)
                if b < 2:
                    TT(x[0:n, b, :], x[0:n, b, :], ps[0:n, WB[b]:WB[b] + 2, :].rearrange("p a n -> p (a n)"), ALU.add)\
                        .then_inc(x2Done, 1)
                else:
                    did(TT(x[0:n, b, 0:512], x[0:n, b, 0:512], ps[0:n, WB[b], :], ALU.add))
                    TT(x[0:n, b, 512:1024], x[0:n, b, 512:1024], ps[64:64 + n, WB[b], :], ALU.add).then_inc(x2Done, 1)

            def norm_rows(b):
                t0, n = TOK[b]
                dve.wait_ge(x2TMM, b + 1)
                if b:
                    dve.wait_ge(lgMM, b)
                dve.tensor_copy(x2T[:, :, 0:n], ps[:, 6:8, :].rearrange("p a (k t) -> p (a k) t", t=128)[:, :, 0:n])\
                    .then_inc(x2TOut, 1)
                dve.wait_ge(root2Done, b + 1)
                need(did(dve.reciprocal(st[0:n, 15 + b:16 + b], st[0:n, 12 + b:13 + b])))
                dve.wait_ge(x2Done, b + 1)
                TS(h2f[0:n, b % 2, :], x[0:n, b, :], st[0:n, 15 + b:16 + b], None, ALU.mult).then_inc(normed, 1)

            def remainders():
                hf = h2f[:, 0, :]
                dve.wait_ge(partDone, 1)
                dve.wait_ge(normed, 1)
                TT(hf, hf, h2p[:, 0, 0, :], ALU.subtract).then_inc(resid, 1)
                dve.wait_ge(partDone, 2)
                dve.wait_ge(resid, 1)
                did(TT(h2p[:, 2, 0, :], hf, h2p[:, 1, 0, :], ALU.subtract), h2Parts)

            def choose(b):
                n = TOK[b][1]
                four = [128, TOPK, E]
                dve.wait_ge(lgMM, b + 1)
                need(did(STT(lg[0:n, b, :], ps[0:n, LGB[b], E * b:E * b + E], st[0:n, 15 + b:16 + b], rb[0:n, :], ALU.mult, ALU.add)))
                need(did(dve.max(mx[0:n, b, :], lg[0:n, b, :])))
                need(did(dve.max_index(mi[0:n, b, :], mx[0:n, b, :], lg[0:n, b, :])))
                did(TS(lg[0:n, b, 0:4], mx[0:n, b, 0:4], mx[0:n, b, 0:1], None, ALU.subtract), mxDone)
                need(did(dve.tensor_copy(mif[0:n, b, :], mi[0:n, b, :])))
                need(did(TT(oh[:, b], expId.unsqueeze(1).broadcast_to(four), mif[:, b, 0:4].unsqueeze(2).broadcast_to(four),
                            ALU.is_equal)))
                dve.tensor_reduce(sel[0:n, b, :], oh[0:n, b].rearrange("p k e -> p e k"), AX.X, ALU.max).then_inc(selDone, 1)

            def weigh(b0, b1):
                nb = b1 - b0
                dve.wait_ge(exDone, b1)
                e_, s_, o_ = ex[:, b0:b1, :], st[:, 18 + b0:18 + b1], oh[:, b0:b1]
                need(did(dve.tensor_reduce(s_, e_, AX.X, ALU.add)))
                need(did(dve.reciprocal(s_, s_)))
                need(did(TT(e_, e_, s_.unsqueeze(2).broadcast_to([128, nb, 4]), ALU.mult)))
                need(did(TT(o_, o_, e_.unsqueeze(3).broadcast_to([128, nb, TOPK, E]), ALU.mult)))
                need(did(dve.tensor_reduce(comb[:, b0:b1, 0:E], o_.rearrange("p b k e -> p b e k"), AX.X, ALU.add)))

            add_mixer(0)
            norm_rows(0)
            remainders()
            add_mixer(1)
            choose(0)
            weigh(0, 1)
            norm_rows(1)
            add_mixer(2)
            choose(1)
            norm_rows(2)
            choose(2)
            for b, (t0, n) in enumerate(TOK):
                dve.wait_ge(posMM, 3)
                dve.wait_ge(selDone, b + 1)
                did(STT(posm[0:n, b, 0:E], ps[0:n, 5, 128 + E * b:128 + E * b + E], 1.0, sel[0:n, b, :], ALU.add, ALU.mult), posOut)
            dve.wait_ge(posOut, 3)
            dve.wait_ge(stOut, 16)
            dve.wait_ge(tailOut, 32)

            def count_rounds():
                need(did(dve.tensor_reduce(cmax[0:1, :], ps[0:1, 5, 256:256 + E], AX.X, ALU.max)))
                need(did(TS(st[0:1, 0:8], roundStart[0:1, :], cmax[0:1, 0:1], None, ALU.is_lt)))
                need(did(dve.tensor_reduce(cmax[0:1, :], st[0:1, 0:8], AX.X, ALU.add)))
                did(dve.tensor_copy(roundsT[0:1, :], cmax[0:1, :]), roundsDone)

            def one_round(r):
                p0, e0 = r * (E + 1), r * E

                def prepare(m, col):
                    dve.wait_ge(xgMM, m + START)
                    for b, (t0, n) in enumerate(TOK):
                        ins = TS(P[0:n, b, :], iota2[0:n, 0:SLOTS], posm[0:n, b, col], None, ALU.is_equal)
                    ins.then_inc(prep, 1)
                    if isinstance(r, int) and isinstance(m, int):
                        weigh(1, 3)
                    dve.wait_ge(gtMM, m + START)
                    for b, (t0, n) in enumerate(TOK):
                        ins = TS(G[0:n, b, :], iota2[0:n, :], posm[0:n, b, col], comb[0:n, b, col], ALU.is_equal, ALU.mult)
                    ins.then_inc(prepG, 1)

                def gathered(m):
                    dve.wait_ge(xgTMM, m + 1 + START)
                    TT(xgT.rearrange("p (c a s) -> p c a s", c=4, a=2),
                       ps[:, 3, :].rearrange("p (c a s) -> p c a s", c=4, a=2),
                       par[:, NF:NF + 8].rearrange("p (a c) -> p c a", a=2).unsqueeze(3).broadcast_to([128, 4, 2, SLOTS]),
                       ALU.mult).then_inc(xgTOut, 1)

                def add_rows(e):
                    for b, (t0, n) in enumerate(TOK):
                        dve.wait_ge(scatMM, e * 3 + (b + 1) + START)
                        dve.wait_ge(accDone, e * 3 + b + START)
                        TT(x[0:n, b, :], x[0:n, b, :], ps[0:n, 6:8, :].rearrange("p a n -> p (a n)"), ALU.add)\
                            .then_inc(accDone, 1)

                dve.wait_ge(posShift, r + START)
                prepare(p0, slice(0, 1))
                if isinstance(r, int):
                    count_rounds()
                    dve.memset(GT[:, 1, :], 0.0)
                    dve.memset(ysb, 0.0).then_inc(zeroed, 1)
                gathered(p0)
                with dve.Fori(0, BODIES) as it:
                    for j in range(PER_BODY):
                        e = e0 + (it * PER_BODY + j)
                        m = p0 + (it * PER_BODY + (j + 1))
                        prepare(m, bass.ds(it * PER_BODY + (j + 1), 1))
                        add_rows(e)
                        dve.wait_ge(wUsed, e * LPE + 4 + START)
                        TS(ga, ps[:, 0, :], LIMIT, None, ALU.min).then_inc(aDone, 1)
                        dve.wait_ge(wUsed, e * LPE + 8 + START)
                        TS(gu, ps[:, 1, :], LIMIT, -LIMIT, ALU.min, ALU.max).then_inc(uDone, 1)
                        dve.wait_ge(aDone, e + 1 + START)
                        dve.wait_ge(uDone, e + 1 + START)
                        STT(gt, gu, 1.0, ga, ALU.add, ALU.mult).then_inc(tDone, 1)
                        dve.wait_ge(sigDone, e + 1 + START)
                        dve.wait_ge(tDone, e + 1 + START)
                        dve.wait_ge(hidTMM, e + START)
                        TT(hid, gt, gs, ALU.mult).then_inc(hidDone, 1)
                        gathered(m)
                dve.wait_ge(prep, p0 + (E + 1) + START)
                dve.sem_inc(aloneV, 1)
                TS(posm[:], posm[:], -float(SLOTS), None, ALU.add).then_inc(posShift, 1)
                dve.wait_ge(accDone, (e0 + E) * 3 + START)
                dve.wait_ge(xgTOut, (r + 1) * (E + 1) + START)
                dve.sem_inc(aloneV, 1)

            one_round(0)
            dve.wait_ge(roundsDone, 1)
            further_rounds(dve, one_round)
            dve.wait_ge(fnwIn, 16)

            def final_scale(b):
                n = TOK[b][1]
                dve.wait_ge(finRoot, b + 1)
                need(did(dve.reciprocal(st[0:n, 6 + b:7 + b], st[0:n, 3 + b:4 + b])))
                STT(yout[0:n, b, :], x[0:n, b, :], st[0:n, 6 + b:7 + b], fnw[0:n], ALU.mult, ALU.mult).then_inc(finDone, 1)

            for b, (t0, n) in enumerate(TOK):
                dve.wait_ge(lastMM, b + 1)
                TT(x[0:n, b, :], x[0:n, b, :], ps[0:n, 2 * b:2 * b + 2, :].rearrange("p a n -> p (a n)"), ALU.add).then_inc(moeDone, 1)
                if b:
                    final_scale(b - 1)
            dve.wait_ge(moeDone, 3)
            final_scale(2)

        @block.tensor
        def _(pe):
            MM, TR = pe.matmul, pe.transpose
            credit(pe, wUsed, xgMM, gtMM, xgTMM, hidTMM, scatMM)
            pe.wait_ge(constIn, 16)
            pe.wait_ge(parIn, 16)
            TR(ps[:, 0, 0:44], parRows[:], ident[0:44, 0:44]).then_inc(parMM, 1)
            for b, (t0, n) in enumerate(TOK):
                pe.wait_ge(scaleDone, b + 1)
                for k in range(KT):
                    ins = MM(ps[:, 2 + 2 * b + k // 4, 128 * (k % 4):128 * (k % 4) + n], x[0:n, b, 128 * k:128 * k + 128],
                             rowScale[0:n, b, 0:n], start=True, stop=True)
                ins.then_inc(xTMM, 1)
            pe.wait_ge(histIn, 16)
            for c in range(4):
                ins = TR(ps[:, 1, 16 * c:16 * c + 16], histRows[0:16, 128 * c:128 * c + 128], ident[0:16, 0:16])
            ins.then_inc(histMM, 1)
            pe.wait_ge(hTOut, 3)
            pe.wait_ge(histOut, 1)
            beside = None
            for at, item in enumerate(SCHED):
                kind = item[0]
                if item in UIDX:
                    n = UIDX[item]
                    l0 = W_CHUNK[kind][0]
                    if n >= 2:
                        pe.wait_ge(unitOut[n % 2], n // 2)
                    if kind == "i":
                        _, c, b = item
                        t0, nt = TOK[b]
                        L = l0 + c
                        pe.wait_ge(ringIn[L % NR], ring_value(L))
                        for k in range(KT):
                            if b < 2:
                                ins = MM(ps[:, n % 2, 0:256], hT[:, k, t0:t0 + nt], slot_k(L, 256)[:, k, :],
                                         start=(k == 0), stop=(k == KT - 1))
                            else:
                                for half in range(2):
                                    ins = MM(ps[64 * half:64 * half + 64, n % 2, 0:256], hT[:, k, t0:t0 + nt],
                                             slot_k(l0 + half, 256)[:, k, :], start=(k == 0), stop=(k == KT - 1))
                    else:
                        L, half = l0 + item[1] // 2, item[1] % 2
                        pe.wait_ge(ringIn[L % NR], ring_value(L))
                        for k in range(KT):
                            if beside:
                                beside(k)
                            ins = MM(ps[:, n % 2, 0:NT], slot_k(L, 256)[:, k, 128 * half:128 * half + 128], hT[:, k, :],
                                     start=(k == 0), stop=(k == KT - 1))
                        beside = None
                    ins.then_inc(projMM, 1)
                elif kind == "lev":
                    _, l, p = item
                    if l == 0:
                        for kk in ("f", "q"):
                            for h in (2 * p, 2 * p + 1):
                                m = UIDX[(kk, h)]
                                pe.wait_ge(unitOut[m % 2], m // 2 + 1)
                        pe.wait_ge(kScaled, 2 * p + 2)
                    else:
                        pe.wait_ge(levOut, 2 * (l - 1) + p + 1)
                    src = q if l == 0 else qP
                    cols = (lambda ap: ap) if l == 0 else lambda ap: later_blocks(ap, l)
                    for hh in range(2):
                        h = 2 * p + hh
                        for b in range(2):
                            ins = MM(cols(ps[:, 2 + h, 128 * b:128 * b + 128]), kS[:, h, 128 * b:128 * b + 128],
                                     cols(src[:, h, 128 * b:128 * b + 128]), start=True, stop=True)
                        if l <= 3:
                            ins = MM(cols(ps[0:64, 2 + h, NP:NT]), kS[:, h, NP:NT], cols(src[:, h, NP:NT]), start=True, stop=True)
                    ins.then_inc(levMM, 1)
                elif kind == "cross":
                    pe.wait_ge(levOut, 2 * (NLEV + 1))
                    for h in range(NH):
                        ins = MM(ps[:, 6, 128 * h:128 * h + 128], kS[:, h, 0:128], qP[:, h, 128:256], start=True, stop=True)
                    ins.then_inc(levMM, 1)
                elif kind == "o":
                    h = item[1]
                    if h == 0:
                        pe.wait_ge(crossOut, 1)
                        pe.wait_ge(s0In, 16)
                    o = ps[:, 2 + h, :]
                    hv = slice(128 * h, 128 * h + 128)
                    MM(o[:, 0:128], v[:, 0, hv], sc[:, h, 0:128], start=True, stop=False, skip_group_check=True)
                    MM(o[:, 128:256], v[:, 0, hv], sc[:, h, 256:384], start=False, stop=False, skip_group_check=True)
                    MM(o[:, 128:256], v[:, 1, hv], sc[:, h, 128:256], start=False, stop=False, skip_group_check=True)
                    MM(o[:, NP:NT], v[0:64, 2, hv], sc[0:64, h, 384:448], start=False, stop=False, skip_group_check=True)

                    def state_part(s, h=h, o=o):
                        t = NP + LS * s
                        ins = MM(o[:, t:t + LS], s0v[:, s, h, :], qP[:, h, t:t + LS], start=False, stop=True, skip_group_check=True)
                        if s == NSEQ - 1:
                            ins.then_inc(oMM, 1)

                    if at + 1 < len(SCHED) and SCHED[at + 1] in UIDX:
                        beside = state_part
                    else:
                        for s in range(NSEQ):
                            state_part(s)
                elif kind == "ss":
                    h = item[1]
                    pe.wait_ge(oSq, h + 1)
                    if h >= 2:
                        pe.wait_ge(oRoot, h - 1)
                    MM(ps[:, 6 + h % 2, 0:NT], ones, sc[:, h, 0:NT], start=True, stop=True).then_inc(ssMM, 1)
                elif kind == "ktok":
                    pe.wait_ge(oRoot, NH)
                    pe.wait_ge(levOut, 2 * (NLEV + 1) + 1)
                    pe.wait_ge(mixDone, 1)
                    for h in range(NH):
                        for b in range(2):
                            TR(ps[:, 6 + h // 2, 256 * (h % 2) + 128 * b:256 * (h % 2) + 128 * b + 128],
                               kS[:, h, 128 * b:128 * b + 128], ident)
                    for h in range(NH):
                        ins = TR(ps[0:64, 2, 128 * h:128 * h + 128], kS[:, h, NP:NT], ident)
                    ins.then_inc(kTokMM, 1)
                elif kind == "stp":
                    pe.wait_ge(kTokOut, 1)
                    pe.wait_ge(mixDone, NH)
                    for h in range(NH):
                        for b in range(2):
                            ins = MM(ps[:, 3, 128 * h:128 * h + 128], kTok[:, 2 * h + b, :], v[:, b, 128 * h:128 * h + 128],
                                     start=(b == 0), stop=(b == 1))
                    ins.then_inc(stPMM, 1)
                elif kind == "sts":
                    h = item[1]
                    pe.wait_ge(vSelDone, h + 1)
                    if h:
                        pe.wait_ge(stSOut, h)
                    for a in range(2):
                        ins = MM(ps[:, 4 + a, :], kTok[0:64, 8 + h, :],
                                 vSel[h % 2][0:64, 4 * a:4 * a + 4, :].rearrange("p b d -> p (b d)"), start=True, stop=True)
                    ins.then_inc(stSMM, 1)

            def tails():
                pe.wait_ge(tailIn, 1)
                for c in range(4):
                    ins = TR(ps[0:18, 7, 128 * c:128 * c + 128], tail[:, c, :], ident)
                ins.then_inc(tailMM, 1)

            def wout(b, k_tiles):
                t0, n = TOK[b]
                for k in k_tiles:
                    L = L_WOUT + k // 2
                    w = slot_k(L, D)[:, k % 2, :]
                    if b == 0 and k % 2 == 0:
                        pe.wait_ge(ringIn[L % NR], ring_value(L))
                    for half in range(2):
                        dst = ps[0:n, 2 * b + half, :] if b < 2 else ps[64 * half:64 * half + 64, 4, :]
                        ins = MM(dst, mixT[:, k, t0:t0 + n], w[:, 512 * half:512 * half + 512], start=(k == 0), stop=(k == KT - 1))
                if k == KT - 1:
                    ins.then_inc(woutMM, 1)

            def turn_x2(b):
                t0, n = TOK[b]
                pe.wait_ge(x2Done, b + 1)
                if b:
                    pe.wait_ge(x2TOut, b)
                else:
                    pe.wait_ge(tailTOut, 1)
                for k in range(KT):
                    ins = TR(ps[:, 6 + k // 4, 128 * (k % 4):128 * (k % 4) + n], x[0:n, b, 128 * k:128 * k + 128], ident[0:n, 0:n])
                ins.then_inc(x2TMM, 1)

            def logits(b):
                t0, n = TOK[b]
                pe.wait_ge(x2TOut, b + 1)
                for k in range(KT):
                    ins = MM(ps[0:n, LGB[b], E * b:E * b + E], x2T[:, k, 0:n], rw[:, k, :], start=(k == 0), stop=(k == KT - 1))
                ins.then_inc(lgMM, 1)

            def positions(b):
                t0, n = TOK[b]
                pe.wait_ge(selDone, b + 1)
                for a in range(b):
                    MM(ps[0:n, 5, 128 + E * b:128 + E * b + E], onesb[:, 0:n], sel[:, a, :], start=(a == 0), stop=False)
                ins = MM(ps[0:n, 5, 128 + E * b:128 + E * b + E], trib[0:n, 0:n], sel[0:n, b, :], start=(b == 0), stop=True)
                if b == 2:
                    for a, (_, na) in enumerate(TOK):
                        ins = MM(ps[:, 5, 256:256 + E], onesb[0:na, :], sel[0:na, a, :], start=(a == 0), stop=(a == 2))
                ins.then_inc(posMM, 1)

            pe.wait_ge(mixDone, NH)
            pe.wait_ge(unitOut[0], UNITS_OF[0])
            pe.wait_ge(unitOut[1], UNITS_OF[1])
            wout(0, range(KT))
            tails()
            pe.wait_ge(stPOut, 1)
            wout(1, range(KT // 2))
            turn_x2(0)
            wout(1, range(KT // 2, KT))
            logits(0)
            pe.wait_ge(stSOut, NH)
            wout(2, range(KT // 2))
            turn_x2(1)
            wout(2, range(KT // 2, KT))
            logits(1)
            turn_x2(2)
            logits(2)
            for b in range(3):
                positions(b)
            pe.wait_ge(h2Parts, 1)
            pe.wait_ge(biasDone, 1)

            def one_round(r):
                p0, e0 = r * (E + 1), r * E

                def gather(m):
                    pe.wait_ge(prep, m + 1 + START)
                    pe.wait_ge(xgTOut, m + START)
                    for b, (t0, n) in enumerate(TOK):
                        if b:
                            pe.wait_ge(h2Parts, b + 1)
                        for part in range(3):
                            for half in range(2):
                                ins = MM(ps[64 * half:64 * half + 64, 3, :], P[0:n, b, :],
                                         h2p[0:n, part, b, 512 * half:512 * half + 512],
                                         start=(b == 0 and part == 0), stop=(b == 2 and part == 2))
                    ins.then_inc(xgMM, 1)

                def turn_gates(m):
                    pe.wait_ge(roundsDone, 1)
                    pe.wait_ge(prepG, m + 1 + START)
                    pe.wait_ge(gtOut, m + START)
                    for b, (t0, n) in enumerate(TOK):
                        ins = TR(ps[:, 5, t0:t0 + n], G[0:n, b, :], ident[0:n, 0:n])
                    ins.then_inc(gtMM, 1)

                def turn(m):
                    pe.wait_ge(xgOut, m + 1 + START)
                    for c in range(4):
                        ins = TR(ps[:, 3, 128 * c:128 * c + 128], xgs[:, 128 * c:128 * c + 128], ident)
                    ins.then_inc(xgTMM, 1)

                def scatter(b, e, par):
                    t0, n = TOK[b]
                    pe.wait_ge(accDone, e * 3 + b + START)
                    if n == 64:
                        pe.sem_inc(aloneT, 1)
                    for half in range(2):
                        ins = MM(ps[0:n, 6 + half, :], GT[64 * half:64 * half + 64, par, t0:t0 + n],
                                 ysb[64 * half:64 * half + 64, :], start=True, stop=True)
                    ins.then_inc(scatMM, 1)

                def product(mat, bank, lhs, e, it, j, between=()):
                    for half in range(2):
                        MM(ps[64 * half:64 * half + 64, bank, :], eh[:, j % 2, :], bias3[:, mat, 512 * half:512 * half + 512],
                           start=True, stop=False)
                    for k in range(KT):
                        n = LPE * j + 4 * mat + k // 2
                        s = (L_EXP + n) % NR
                        if k % 2 == 0:
                            pe.wait_ge(ringIn[s], (r * BODIES + it) * (16 * PER_BODY * LPE // NR) + ring_value(L_EXP + n))
                        w = ring[:, s, D * (k % 2):D * (k % 2) + D]
                        for half in range(2):
                            ins = MM(ps[64 * half:64 * half + 64, bank, :], lhs(k), w[:, 512 * half:512 * half + 512],
                                     start=False, stop=(k == KT - 1))
                        if k % 2:
                            ins.then_inc(wUsed, 1)
                            if k // 2 < len(between):
                                between[k // 2]()

                half_c = lambda ap: (lambda k: ap[:, 128 * (k % 4) + 64 * (k // 4):128 * (k % 4) + 64 * (k // 4) + 64])
                gather(p0)
                turn_gates(p0)
                turn(p0)
                pe.wait_ge(zeroed, 1)
                with pe.Fori(0, BODIES) as it:
                    for j in range(PER_BODY):
                        e = e0 + (it * PER_BODY + j)
                        m0 = p0 + (it * PER_BODY + j)
                        m = p0 + (it * PER_BODY + (j + 1))

                        def scatter_before(b, e=e, m0=m0, j=j):
                            if b == 0:
                                pe.wait_ge(yEvac, e + START)
                                pe.wait_ge(gtOut, m0 + START)
                            scatter(b, e, (j + 1) % 2)

                        pe.wait_ge(ehDone, m + START)
                        pe.wait_ge(xgTOut, m + START)
                        pe.wait_ge(aDone, e + START)
                        product(0, 0, half_c(xgT), e, it, j, [lambda b=b: scatter_before(b) for b in range(3)])
                        pe.wait_ge(uDone, e + START)
                        product(1, 1, half_c(xgT), e, it, j)
                        gather(m)
                        turn_gates(m)
                        pe.wait_ge(hidDone, e + 1 + START)
                        pe.wait_ge(hidTOut, e + START)
                        for c in range(4):
                            ins = TR(ps[:, 4, 128 * c:128 * c + 128], hid[:, 128 * c:128 * c + 128], ident)
                        ins.then_inc(hidTMM, 1)
                        turn(m)
                        pe.wait_ge(hidTOut, e + 1 + START)
                        pe.wait_ge(yEvac, e + START)
                        product(2, 2, half_c(hidT), e, it, j)
                pe.wait_ge(yEvac, e0 + E + START)
                pe.wait_ge(accDone, (e0 + E) * 3 + START)
                pe.wait_ge(xgTOut, p0 + (E + 1) + START)
                pe.wait_ge(gtOut, p0 + (E + 1) + START)
                pe.sem_inc(aloneT, 1)

            one_round(0)
            pe.wait_ge(roundsDone, 1)
            further_rounds(pe, one_round)
            for b, (t0, n) in enumerate(TOK):
                for half in range(2):
                    ins = MM(ps[0:n, 2 * b + half, :], GT[64 * half:64 * half + 64, 1, t0:t0 + n], ysb[64 * half:64 * half + 64, :],
                             start=True, stop=True)
                ins.then_inc(lastMM, 1)


_IN = ["x_prompt", "x_sample", "state_conv", "state_hgrn", "w_in", "w_out", "router_w", "router_b", "w_gate", "b_gate",
       "w_up", "b_up", "w_down", "b_down", "final_norm_w"]
_ROWS = ["lb_logits", "conv_w", "conv_b", "gnorm_w", "norm_mix_w", "norm_ffn_w"]
_OUT = [("y_prompt", (1, 256, 1024)), ("y_sample", (8, 8, 1024)), ("new_conv_prompt", (1, 1, 2, 512)),
        ("new_hgrn_prompt", (1, 1, 4, 128, 128)), ("new_conv_sample", (1, 8, 2, 512)),
        ("new_hgrn_sample", (1, 8, 4, 128, 128))]


def _constants():
    import numpy as np
    p = np.arange(128)
    slots = np.tile(np.arange(1, 65), 2)
    pick = (p[:, None] % 32 == np.arange(34)[None]) & (p[:, None] // 32 != 1)
    parts = [np.eye(128), p[:, None] < p[None], np.ones((128, 128)), np.broadcast_to(slots, (128, 128)), pick,
             np.broadcast_to(64 * np.arange(8), (128, 8)), p[:, None] // 8 == np.arange(8)[None],
             np.broadcast_to(np.arange(32), (128, 32))]
    consts = np.ascontiguousarray(np.concatenate([a.astype(np.float32) for a in parts], axis=1))
    s, t = p[:, None], p[None]
    lev = [(s // (2 * n) == t // (2 * n)) & (s // n % 2 == 0) & (t // n % 2 == 1) for n in (1, 2, 4, 8, 16, 32, 64)]
    return consts, np.ascontiguousarray(np.stack(lev, axis=1).astype(np.float32))


def kernel(**inputs):
    import numpy as np
    import concourse.bacc as bacc
    from concourse.bass_utils import run_bass_kernel_spmd

    nc = bacc.Bacc("TRN2", target_bir_lowering=False, num_devices=1)
    arrays = {n: np.ascontiguousarray(inputs[n]) for n in _IN}
    arrays["par_rows"] = np.concatenate([np.ascontiguousarray(inputs[n]).reshape(-1, 128) for n in _ROWS])
    arrays["consts"], arrays["lev_mask"] = _constants()
    aps = {n: nc.dram_tensor("in_" + n, a.shape, mybir.dt.from_np(a.dtype), kind="ExternalInput").ap()
           for n, a in arrays.items()}
    for n, shape in _OUT:
        aps[n] = nc.dram_tensor(n, shape, mybir.dt.float32, kind="ExternalOutput").ap()
    hybrid_shortconv_hgrn2_moe_step(nc, aps)
    r = run_bass_kernel_spmd(nc, [{"in_" + n: a for n, a in arrays.items()}], core_ids=[0])
    return tuple(r.results[0][n] for n, _ in _OUT)
```
